# Optimizing a Trainium2 kernel written in Bass

```python
import math
import jax, jax.numpy as jnp
from jax import lax
import numpy as np

D_MODEL = 1024
BATCH = 1
SEQ = 256
DEPTH = 2

N_MEM = 256
MIX_HALF = D_MODEL // 2
A_HEADS = 4
A_HEAD_DIM = MIX_HALF // A_HEADS
DILATED_GROUPS = ((128, 1), (512, 4), (2048, 16))
PAD_MULTIPLE = 2048
RG_WIDTH = MIX_HALF
RG_BLOCKS = 4
RG_BLOCK_DIM = RG_WIDTH // RG_BLOCKS
RG_C = 8.0
CONV_WIDTH = 4
POOL_WINDOWS = (2, 4, 8, 16)
POOL_GROUP_DIM = D_MODEL // len(POOL_WINDOWS)
XA_HEADS = 4
XA_HEAD_DIM = D_MODEL // XA_HEADS
D_FF = 4 * D_MODEL
IN_COLS = 3 * MIX_HALF + 2 * RG_WIDTH
N_EVEN = (DEPTH + 1) // 2
N_ODD = DEPTH // 2
EPS = 1e-6


def rms_norm(x, g):
    xf = x.astype(jnp.float32)
    y = xf * lax.rsqrt(jnp.mean(xf * xf, axis=-1, keepdims=True) + EPS)
    return (y * g.astype(jnp.float32)).astype(x.dtype)

def dilated_window_attn(q, k, v, window, dilation):
    B, S, H, C = q.shape
    L = window // dilation
    nb = S // window

    def split(t):
        return t.reshape(B, nb, L, dilation, H, C)

    def with_prev(t):
        prev = jnp.pad(t, ((0, 0), (1, 0), (0, 0), (0, 0), (0, 0), (0, 0)))[:, :-1]
        return jnp.concatenate([prev, t], axis=2)

    qb = split(q)
    kc = with_prev(split(k))
    vc = with_prev(split(v))
    s = jnp.einsum('bnqrhc,bnkrhc->bnrhqk', qb, kc).astype(jnp.float32) * (C ** -0.5)
    qi = jnp.arange(L)[:, None]
    kj = jnp.arange(2 * L)[None, :]
    dist = qi + L - kj
    band = (dist >= 0) & (dist <= L)
    first = (jnp.arange(nb) == 0)[:, None, None]
    mask = band[None] & (jnp.logical_not(first) | (kj >= L)[None])
    s = jnp.where(mask[None, :, None, None], s, -jnp.inf)
    m = jnp.max(s, axis=-1, keepdims=True)
    p = jnp.exp(s - m)
    den = jnp.sum(p, axis=-1)
    o = jnp.einsum('bnrhqk,bnkrhc->bnqrhc', p, vc.astype(jnp.float32))
    den_t = den.transpose(0, 1, 4, 2, 3)
    o = o / den_t[..., None]
    lse = m[..., 0].transpose(0, 1, 4, 2, 3) + jnp.log(den_t)
    return o.reshape(B, S, H, C), lse.reshape(B, S, H)

def mixer_attn_rglru(h, w_in, q_g, k_g, conv_w, conv_b, ga_w, ga_b, gx_w, gx_b, lam, w_out):
    B, S, _ = h.shape
    proj = h @ w_in
    q, k, v, xr, gate = jnp.split(
        proj, [MIX_HALF, 2 * MIX_HALF, 3 * MIX_HALF, 3 * MIX_HALF + RG_WIDTH], axis=-1)

    q = rms_norm(q.reshape(B, S, A_HEADS, A_HEAD_DIM), q_g)
    k = rms_norm(k.reshape(B, S, A_HEADS, A_HEAD_DIM), k_g)
    v = v.reshape(B, S, A_HEADS, A_HEAD_DIM)
    Sp = -(-S // PAD_MULTIPLE) * PAD_MULTIPLE
    pad = ((0, 0), (0, Sp - S), (0, 0), (0, 0))
    qp, kp, vp = jnp.pad(q, pad), jnp.pad(k, pad), jnp.pad(v, pad)
    outs, lses = [], []
    for window, dilation in DILATED_GROUPS:
        o_g, lse_g = dilated_window_attn(qp, kp, vp, window, dilation)
        outs.append(o_g)
        lses.append(lse_g)
    wts = jax.nn.softmax(jnp.stack(lses), axis=0)
    o_a = jnp.sum(wts[..., None] * jnp.stack(outs), axis=0)[:, :S]
    o_a = o_a.reshape(B, S, MIX_HALF).astype(h.dtype)

    xpad = jnp.pad(xr, ((0, 0), (CONV_WIDTH - 1, 0), (0, 0)))
    xc = conv_b + sum(xpad[:, j:j + S] * conv_w[j] for j in range(CONV_WIDTH))
    xb = xc.reshape(B, S, RG_BLOCKS, RG_BLOCK_DIM)
    r = jax.nn.sigmoid(jnp.einsum('bsgc,gcd->bsgd', xb, ga_w).reshape(B, S, RG_WIDTH) + ga_b)
    i = jax.nn.sigmoid(jnp.einsum('bsgc,gcd->bsgd', xb, gx_w).reshape(B, S, RG_WIDTH) + gx_b)
    log_a = -RG_C * r.astype(jnp.float32) * jax.nn.softplus(-lam.astype(jnp.float32))
    a = jnp.exp(log_a)
    u = jnp.sqrt(-jnp.expm1(2.0 * log_a)) * (i * xc).astype(jnp.float32)

    def combine(e1, e2):
        a1, b1 = e1
        a2, b2 = e2
        return a1 * a2, a2 * b1 + b2

    _, hs = lax.associative_scan(combine, (a, u), axis=1)
    y_b = hs.astype(h.dtype) * jax.nn.gelu(gate)

    return jnp.concatenate([o_a, y_b], axis=-1) @ w_out

def pool_mixer(h, pool_w, scale):
    B, S, D = h.shape
    hf = h.astype(jnp.float32)
    cs = jnp.pad(jnp.cumsum(hf, axis=1), ((0, 0), (1, 0), (0, 0)))
    t = jnp.arange(S)
    diffs = []
    for g, w in enumerate(POOL_WINDOWS):
        sl = slice(g * POOL_GROUP_DIM, (g + 1) * POOL_GROUP_DIM)
        lo = jnp.maximum(t + 1 - w, 0)
        window_sum = cs[:, 1:, sl] - cs[:, lo, sl]
        count = jnp.minimum(t + 1, w).astype(jnp.float32)[None, :, None]
        diffs.append(window_sum / count - hf[..., sl])
    d = jnp.stack(diffs, axis=2)
    out = jnp.einsum('bsgc,gcd->bsgd', d, pool_w.astype(jnp.float32)).reshape(B, S, D)
    return (out * scale.astype(jnp.float32)).astype(h.dtype)

def memory_xattn(h, mem_n, w_q, w_kv, q_g, k_g, w_o):
    B, S, D = h.shape
    M = mem_n.shape[1]
    q = rms_norm((h @ w_q).reshape(B, S, XA_HEADS, XA_HEAD_DIM), q_g)
    k, v = jnp.split(mem_n @ w_kv, 2, axis=-1)
    k = rms_norm(k.reshape(B, M, XA_HEADS, XA_HEAD_DIM), k_g)
    v = v.reshape(B, M, XA_HEADS, XA_HEAD_DIM)
    s = jnp.einsum('bshc,bmhc->bhsm', q, k).astype(jnp.float32) * (XA_HEAD_DIM ** -0.5)
    p = jax.nn.softmax(s, axis=-1)
    o = jnp.einsum('bhsm,bmhc->bshc', p, v.astype(jnp.float32)).astype(h.dtype)
    return o.reshape(B, S, D) @ w_o

def sq_relu_mlp(h, w1, w2):
    return jnp.square(jax.nn.relu(h @ w1)) @ w2

def first_inputs(seed: int = 0) -> dict:
    key = jax.random.key(seed)
    ks = jax.random.split(key, 26)
    f32 = jnp.float32

    def nrm(k, shape, fan_in):
        return jax.random.normal(k, shape, f32) * fan_in ** -0.5

    def gain(k, shape):
        return 1.0 + 0.02 * jax.random.normal(k, shape, f32)

    def bias(k, shape):
        return 0.02 * jax.random.normal(k, shape, f32)

    u = jax.random.uniform(ks[15], (N_EVEN, RG_WIDTH), f32, minval=0.9, maxval=0.999)
    s = u ** (1.0 / RG_C)
    lam = jnp.log(s) - jnp.log1p(-s)
    return {
        'x': jax.random.normal(ks[0], (BATCH, SEQ, D_MODEL), f32),
        'mem': jax.random.normal(ks[1], (BATCH, N_MEM, D_MODEL), f32),
        'mem_norm_g': gain(ks[2], (D_MODEL,)),
        'mix_norm_g': gain(ks[3], (DEPTH, D_MODEL)),
        'xattn_norm_g': gain(ks[4], (DEPTH, D_MODEL)),
        'mlp_norm_g': gain(ks[5], (DEPTH, D_MODEL)),
        'ev_w_in': nrm(ks[6], (N_EVEN, D_MODEL, IN_COLS), D_MODEL),
        'ev_q_norm_g': gain(ks[7], (N_EVEN, A_HEAD_DIM)),
        'ev_k_norm_g': gain(ks[8], (N_EVEN, A_HEAD_DIM)),
        'ev_conv_w': nrm(ks[9], (N_EVEN, CONV_WIDTH, RG_WIDTH), CONV_WIDTH),
        'ev_conv_b': bias(ks[10], (N_EVEN, RG_WIDTH)),
        'ev_gate_a_w': nrm(ks[11], (N_EVEN, RG_BLOCKS, RG_BLOCK_DIM, RG_BLOCK_DIM), RG_BLOCK_DIM),
        'ev_gate_a_b': bias(ks[12], (N_EVEN, RG_WIDTH)),
        'ev_gate_x_w': nrm(ks[13], (N_EVEN, RG_BLOCKS, RG_BLOCK_DIM, RG_BLOCK_DIM), RG_BLOCK_DIM),
        'ev_gate_x_b': bias(ks[14], (N_EVEN, RG_WIDTH)),
        'ev_lambda': lam,
        'ev_w_out': nrm(ks[16], (N_EVEN, 2 * MIX_HALF, D_MODEL), 2 * MIX_HALF),
        'od_pool_w': nrm(ks[17], (N_ODD, len(POOL_WINDOWS), POOL_GROUP_DIM, POOL_GROUP_DIM), POOL_GROUP_DIM),
        'od_scale': 0.5 + 0.05 * jax.random.normal(ks[18], (N_ODD, D_MODEL), f32),
        'xa_w_q': nrm(ks[19], (DEPTH, D_MODEL, D_MODEL), D_MODEL),
        'xa_w_kv': nrm(ks[20], (DEPTH, D_MODEL, 2 * D_MODEL), D_MODEL),
        'xa_q_norm_g': gain(ks[21], (DEPTH, XA_HEAD_DIM)),
        'xa_k_norm_g': gain(ks[22], (DEPTH, XA_HEAD_DIM)),
        'xa_w_o': nrm(ks[23], (DEPTH, D_MODEL, D_MODEL), D_MODEL),
        'mlp_w1': nrm(ks[24], (DEPTH, D_MODEL, D_FF), D_MODEL),
        'mlp_w2': nrm(ks[25], (DEPTH, D_FF, D_MODEL), D_FF),
    }

def first_block(x, mem, mem_norm_g, mix_norm_g, xattn_norm_g, mlp_norm_g,
              ev_w_in, ev_q_norm_g, ev_k_norm_g, ev_conv_w, ev_conv_b,
              ev_gate_a_w, ev_gate_a_b, ev_gate_x_w, ev_gate_x_b, ev_lambda, ev_w_out,
              od_pool_w, od_scale,
              xa_w_q, xa_w_kv, xa_q_norm_g, xa_k_norm_g, xa_w_o,
              mlp_w1, mlp_w2):
    mem_n = rms_norm(mem, mem_norm_g)
    for l in range(DEPTH):
        h = rms_norm(x, mix_norm_g[l])
        if l % 2 == 0:
            e = l // 2
            x = x + mixer_attn_rglru(h, ev_w_in[e], ev_q_norm_g[e], ev_k_norm_g[e],
                                     ev_conv_w[e], ev_conv_b[e], ev_gate_a_w[e], ev_gate_a_b[e],
                                     ev_gate_x_w[e], ev_gate_x_b[e], ev_lambda[e], ev_w_out[e])
        else:
            o = l // 2
            x = x + pool_mixer(h, od_pool_w[o], od_scale[o])
        x = x + memory_xattn(rms_norm(x, xattn_norm_g[l]), mem_n, xa_w_q[l], xa_w_kv[l],
                             xa_q_norm_g[l], xa_k_norm_g[l], xa_w_o[l])
        x = x + sq_relu_mlp(rms_norm(x, mlp_norm_g[l]), mlp_w1[l], mlp_w2[l])
    return x


MEM_LEN = 256
HEAD_DIM = 64
N_CONV_GROUPS = 6
CONV_CH = N_CONV_GROUPS * HEAD_DIM
CONV_WIDTH_2 = 31
N_Q_HEADS = 6
N_KV_HEADS = 2
SWA_Q = N_Q_HEADS * HEAD_DIM
SWA_KV = N_KV_HEADS * HEAD_DIM
WINDOW = 128
BLOCK = 128
N_MEM_HEADS = 4
MEM_W = N_MEM_HEADS * HEAD_DIM
D_MIX = CONV_CH + SWA_Q + MEM_W
D_IN = 2 * CONV_CH + SWA_Q + 2 * SWA_KV + MEM_W
D_FF_2 = 2816
ROPE_THETA = 10000.0


def rms_norm_2(x, g):
    xf = x.astype(jnp.float32)
    y = xf * lax.rsqrt(jnp.mean(xf * xf, axis=-1, keepdims=True) + EPS)
    return (y * g.astype(jnp.float32)).astype(x.dtype)

def layer_norm(x, g, b):
    xf = x.astype(jnp.float32)
    mu = jnp.mean(xf, axis=-1, keepdims=True)
    var = jnp.mean(jnp.square(xf - mu), axis=-1, keepdims=True)
    y = (xf - mu) * lax.rsqrt(var + EPS)
    return (y * g.astype(jnp.float32) + b.astype(jnp.float32)).astype(x.dtype)

def swiglu(x, w1, w3, w2):
    return (jax.nn.silu(x @ w1) * (x @ w3)) @ w2

def rope_tables(positions):
    inv_freq = ROPE_THETA ** (-jnp.arange(0, HEAD_DIM, 2, dtype=jnp.float32) / HEAD_DIM)
    ang = positions.astype(jnp.float32)[..., None] * inv_freq
    return jnp.cos(ang)[:, :, None, :], jnp.sin(ang)[:, :, None, :]

def apply_rope(x, cos, sin):
    xf = x.astype(jnp.float32)
    x1, x2 = jnp.split(xf, 2, axis=-1)
    out = jnp.concatenate([x1 * cos - x2 * sin, x2 * cos + x1 * sin], axis=-1)
    return out.astype(x.dtype)

def conv_module(u, w_dw, b_dw, ln_g, ln_b):
    a, gate = jnp.split(u, 2, axis=-1)
    y = a * jax.nn.sigmoid(gate)
    y = lax.conv_general_dilated(
        y, w_dw[:, None, :], window_strides=(1,),
        padding=[(CONV_WIDTH_2 - 1, 0)],
        dimension_numbers=('NWC', 'WIO', 'NWC'),
        feature_group_count=CONV_CH) + b_dw
    y = layer_norm(y, ln_g, ln_b)
    return jax.nn.silu(y)

def sliding_window_attention(q, k, v, sinks):
    B, S, _, Dh = q.shape
    nb = S // BLOCK
    g = N_Q_HEADS // N_KV_HEADS
    qb = q.reshape(B, nb, BLOCK, N_KV_HEADS, g, Dh)
    kb = k.reshape(B, nb, BLOCK, N_KV_HEADS, Dh)
    vb = v.reshape(B, nb, BLOCK, N_KV_HEADS, Dh)

    def with_prev(t):
        prev = jnp.concatenate([jnp.zeros_like(t[:, :1]), t[:, :-1]], axis=1)
        return jnp.concatenate([prev, t], axis=2)

    kw, vw = with_prev(kb), with_prev(vb)
    scores = jnp.einsum('bnqhgd,bnkhd->bnhgqk', qb, kw).astype(jnp.float32) * (Dh ** -0.5)
    qi = jnp.arange(BLOCK)[:, None] + BLOCK
    kj = jnp.arange(2 * BLOCK)[None, :]
    rel = qi - kj
    band = (rel >= 0) & (rel < WINDOW)
    first_ok = (jnp.arange(nb)[:, None, None] > 0) | (kj[None] >= BLOCK)
    mask = band[None] & first_ok
    scores = jnp.where(mask[None, :, None, None], scores, -jnp.inf)
    sink = jnp.broadcast_to(
        sinks.astype(jnp.float32).reshape(N_KV_HEADS, g)[None, None, :, :, None, None],
        scores.shape[:-1] + (1,))
    probs = jax.nn.softmax(jnp.concatenate([scores, sink], axis=-1), axis=-1)[..., :-1]
    out = jnp.einsum('bnhgqk,bnkhd->bnqhgd', probs.astype(v.dtype), vw)
    return out.reshape(B, S, N_Q_HEADS * Dh)

def memory_attention(q, mk, mv):
    B, S, _, Dh = q.shape
    scores = jnp.einsum('bshd,bmhd->bhsm', q, mk).astype(jnp.float32) * (Dh ** -0.5)
    probs = jax.nn.softmax(scores, axis=-1)
    out = jnp.einsum('bhsm,bmhd->bshd', probs.astype(mv.dtype), mv)
    return out.reshape(B, S, N_MEM_HEADS * Dh)

def second_inputs(seed: int = 0) -> dict:
    key = jax.random.key(seed)
    ks = iter(jax.random.split(key, 32))
    f32 = jnp.float32

    def w(shape, fan_in):
        return jax.random.normal(next(ks), shape, f32) * (fan_in ** -0.5)

    def gain(shape):
        return 1.0 + 0.02 * jax.random.normal(next(ks), shape, f32)

    def bias(shape):
        return 0.02 * jax.random.normal(next(ks), shape, f32)

    L = DEPTH
    x = jax.random.normal(next(ks), (BATCH, SEQ, D_MODEL), f32)
    mem = jax.random.normal(next(ks), (BATCH, MEM_LEN, D_MODEL), f32)
    positions = jnp.broadcast_to(jnp.arange(SEQ, dtype=jnp.int32)[None, :], (BATCH, SEQ))
    return {
        "x": x,
        "mem": mem,
        "positions": positions,
        "ffn1_norm": gain((L, D_MODEL)),
        "ffn1_w1": w((L, D_MODEL, D_FF_2), D_MODEL),
        "ffn1_w3": w((L, D_MODEL, D_FF_2), D_MODEL),
        "ffn1_w2": w((L, D_FF_2, D_MODEL), D_FF_2),
        "mix_norm": gain((L, D_MODEL)),
        "w_in": w((L, D_MODEL, D_IN), D_MODEL),
        "conv_w": w((L, CONV_WIDTH_2, CONV_CH), CONV_WIDTH_2),
        "conv_b": bias((L, CONV_CH)),
        "conv_ln_g": gain((L, CONV_CH)),
        "conv_ln_b": bias((L, CONV_CH)),
        "swa_q_norm": gain((L, HEAD_DIM)),
        "swa_k_norm": gain((L, HEAD_DIM)),
        "swa_sinks": jax.random.normal(next(ks), (L, N_Q_HEADS), f32),
        "mem_norm": gain((L, D_MODEL)),
        "w_mem_kv": w((L, D_MODEL, 2 * MEM_W), D_MODEL),
        "mem_q_norm": gain((L, HEAD_DIM)),
        "mem_k_norm": gain((L, HEAD_DIM)),
        "w_out": w((L, D_MIX, D_MODEL), D_MIX),
        "ffn2_norm": gain((L, D_MODEL)),
        "ffn2_w1": w((L, D_MODEL, D_FF_2), D_MODEL),
        "ffn2_w3": w((L, D_MODEL, D_FF_2), D_MODEL),
        "ffn2_w2": w((L, D_FF_2, D_MODEL), D_FF_2),
        "final_norm": gain((L, D_MODEL)),
    }

def second_block(x, mem, positions, ffn1_norm, ffn1_w1, ffn1_w3, ffn1_w2, mix_norm, w_in,
              conv_w, conv_b, conv_ln_g, conv_ln_b, swa_q_norm, swa_k_norm, swa_sinks,
              mem_norm, w_mem_kv, mem_q_norm, mem_k_norm, w_out,
              ffn2_norm, ffn2_w1, ffn2_w3, ffn2_w2, final_norm):
    B, S, _ = x.shape
    cos, sin = rope_tables(positions)
    splits = [2 * CONV_CH, 2 * CONV_CH + SWA_Q, 2 * CONV_CH + SWA_Q + SWA_KV,
              2 * CONV_CH + SWA_Q + 2 * SWA_KV]
    for l in range(DEPTH):
        h = x + 0.5 * swiglu(rms_norm_2(x, ffn1_norm[l]), ffn1_w1[l], ffn1_w3[l], ffn1_w2[l])

        n = rms_norm_2(h, mix_norm[l])
        p = n @ w_in[l]
        u_conv, q, k, v, q_mem = jnp.split(p, splits, axis=-1)

        y_conv = conv_module(u_conv, conv_w[l], conv_b[l], conv_ln_g[l], conv_ln_b[l])

        q = apply_rope(rms_norm_2(q.reshape(B, S, N_Q_HEADS, HEAD_DIM), swa_q_norm[l]), cos, sin)
        k = apply_rope(rms_norm_2(k.reshape(B, S, N_KV_HEADS, HEAD_DIM), swa_k_norm[l]), cos, sin)
        v = v.reshape(B, S, N_KV_HEADS, HEAD_DIM)
        y_swa = sliding_window_attention(q, k, v, swa_sinks[l])

        mkv = rms_norm_2(mem, mem_norm[l]) @ w_mem_kv[l]
        mk, mv = jnp.split(mkv, 2, axis=-1)
        mk = rms_norm_2(mk.reshape(B, MEM_LEN, N_MEM_HEADS, HEAD_DIM), mem_k_norm[l])
        mv = mv.reshape(B, MEM_LEN, N_MEM_HEADS, HEAD_DIM)
        qm = rms_norm_2(q_mem.reshape(B, S, N_MEM_HEADS, HEAD_DIM), mem_q_norm[l])
        y_mem = memory_attention(qm, mk, mv)

        y = jnp.concatenate([y_conv, y_swa, y_mem], axis=-1)
        h = h + y @ w_out[l]

        h = h + 0.5 * swiglu(rms_norm_2(h, ffn2_norm[l]), ffn2_w1[l], ffn2_w3[l], ffn2_w2[l])

        x = rms_norm_2(h, final_norm[l])
    return x


def setup_inputs(seed=0):
    out = dict(first_inputs(seed))
    for name, value in second_inputs(seed + 1).items():
        if name != "x":
            out[name + "_2"] = value
    return out


def reference(
    x, mem, mem_norm_g, mix_norm_g, xattn_norm_g, mlp_norm_g, ev_w_in, ev_q_norm_g, ev_k_norm_g,
    ev_conv_w, ev_conv_b, ev_gate_a_w, ev_gate_a_b, ev_gate_x_w, ev_gate_x_b, ev_lambda,
    ev_w_out, od_pool_w, od_scale, xa_w_q, xa_w_kv, xa_q_norm_g, xa_k_norm_g, xa_w_o, mlp_w1,
    mlp_w2, mem_2, positions_2, ffn1_norm_2, ffn1_w1_2, ffn1_w3_2, ffn1_w2_2, mix_norm_2,
    w_in_2, conv_w_2, conv_b_2, conv_ln_g_2, conv_ln_b_2, swa_q_norm_2, swa_k_norm_2,
    swa_sinks_2, mem_norm_2, w_mem_kv_2, mem_q_norm_2, mem_k_norm_2, w_out_2, ffn2_norm_2,
    ffn2_w1_2, ffn2_w3_2, ffn2_w2_2, final_norm_2,
):
    x = first_block(
        x, mem, mem_norm_g, mix_norm_g, xattn_norm_g, mlp_norm_g, ev_w_in, ev_q_norm_g,
        ev_k_norm_g, ev_conv_w, ev_conv_b, ev_gate_a_w, ev_gate_a_b, ev_gate_x_w, ev_gate_x_b,
        ev_lambda, ev_w_out, od_pool_w, od_scale, xa_w_q, xa_w_kv, xa_q_norm_g, xa_k_norm_g,
        xa_w_o, mlp_w1, mlp_w2,
    )
    return second_block(
        x, mem_2, positions_2, ffn1_norm_2, ffn1_w1_2, ffn1_w3_2, ffn1_w2_2, mix_norm_2, w_in_2,
        conv_w_2, conv_b_2, conv_ln_g_2, conv_ln_b_2, swa_q_norm_2, swa_k_norm_2, swa_sinks_2,
        mem_norm_2, w_mem_kv_2, mem_q_norm_2, mem_k_norm_2, w_out_2, ffn2_norm_2, ffn2_w1_2,
        ffn2_w3_2, ffn2_w2_2, final_norm_2,
    )


_drawn_inputs = setup_inputs


def setup_inputs(seed=0):
    import zlib

    import numpy as np

    out = dict(_drawn_inputs(seed))
    spreads = {}
    factors = {'mem_norm_g': 8.0,
     'mix_norm_g': 4.711,
     'xattn_norm_g': 8.0,
     'ev_q_norm_g': 8.0,
     'ev_k_norm_g': 8.0,
     'ev_gate_a_b': 8.0,
     'ev_gate_x_b': 8.0,
     'xa_q_norm_g': 8.0,
     'xa_k_norm_g': 8.0,
     'ffn1_norm_2': 5.941,
     'mix_norm_2': 5.474,
     'conv_b_2': 3.491,
     'conv_ln_g_2': 18.051,
     'conv_ln_b_2': 21.975,
     'swa_q_norm_2': 8.0,
     'swa_k_norm_2': 8.0,
     'swa_sinks_2': 32.4,
     'mem_norm_2': 8.0,
     'mem_q_norm_2': 8.0,
     'mem_k_norm_2': 8.0,
     'ffn2_norm_2': 6.538}
    for name, (base, spread) in spreads.items():
        noise = np.random.default_rng([zlib.crc32(name.encode()), seed]).standard_normal(out[name].shape)
        drawn = base * np.exp(spread * noise) if base else spread * noise
        out[name] = __import__('jax').numpy.asarray(drawn.astype(out[name].dtype))
    for name, factor in factors.items():
        out[name] = (out[name] * factor).astype(out[name].dtype)
    return out
```

```python
from contextlib import ExitStack

import concourse.bass as bass
from concourse import mybir
import numpy as np

F32, F32R, I32 = mybir.dt.float32, mybir.dt.float32r, mybir.dt.int32
ACT, ALU, AX = mybir.ActivationFunctionType, mybir.AluOpType, mybir.AxisListType

P = 128
S, D = 256, 1024
NT, KC = S // P, D // P
EPS = 1e-6
UNIT = 2048
SLOTS = 3
AHEAD = SLOTS - 1
D_FF, D_FF2 = 4096, 2816
FF = 256
PARTIAL = 768
BIG = -1e30

def _columns(widths):
    at, out = 0, {}
    for name, w in widths:
        out[name] = slice(at, at + w)
        at += w
    return out, at

SMALL, N_SMALL = _columns([
    ("mem_g", KC), ("mix_g0", KC), ("mix_g1", KC), ("xat_g0", KC), ("xat_g1", KC), ("mlp_g0", KC), ("mlp_g1", KC),
    ("ev_q", 4), ("ev_k", 4), ("conv_w", 16), ("conv_b", 4), ("ga_b", 4), ("gx_b", 4), ("lam", 4),
    ("xq0", 4), ("xq1", 4), ("xk0", 4), ("xk1", 4)])
LAYER, N_LAYER = _columns([
    ("ffn1_g", KC), ("mix_g", KC), ("mem_g", KC), ("ffn2_g", KC), ("conv_w", 93), ("conv_b", 3), ("ln_g", 3),
    ("ln_b", 3), ("sinks", 6), ("mq_g", 2), ("mk_g", 2), ("qk_g", 512), ("final_g", D)])
CONST, N_CONST = _columns([("ident", P), ("ones", P), ("neg1", 512), ("cnt", 512), ("neg2", 512), ("freq", 32)])


class Count:

    def __init__(self, base=0, steps=None):
        self.base, self.steps = base, dict(steps or {})

    def plus(self, n):
        return Count(self.base + n, self.steps)

    def same_steps(self, other):
        return self.steps == other.steps


class Lane:

    def __init__(self, prog, name, eng):
        self.prog, self.name, self.eng, self.seen = prog, name, eng, {}

    def after(self, *tokens):
        need = {}
        for sem, value in tokens:
            best = need.get(sem)
            if best is None or (best.same_steps(value) and value.base > best.base):
                need[sem] = value
            elif not best.same_steps(value):
                self._wait(sem, value)
        for sem, value in need.items():
            self._wait(sem, value)
        return self.eng

    def _wait(self, sem, value):
        known = self.seen.get(sem)
        if known is not None and known.same_steps(value) and known.base >= value.base:
            return
        if not value.steps and value.base <= 0:
            return
        self.seen[sem] = value
        self.eng.wait_ge(self.prog.sems[sem], self.prog.value(value, self.eng))

    def did(self, inst, sem=None, n=1):
        sem = sem or self.name
        inst.then_inc(self.prog.sems[sem], n)
        self.prog.counts[sem] = self.prog.counts[sem].plus(n)
        return (sem, self.prog.counts[sem])


class Program:

    def __init__(self, nc, sems, steps):
        self.nc, self.sems, self.steps = nc, sems, steps
        self.counts = {s: Count() for s in sems}
        self.counts["unit"] = Count()
        self.live, self.vars, self.n_loops = {}, {}, 0
        self.lanes = []

    def value(self, count, eng=None):
        v = count.base
        for var, step in count.steps.items():
            v = self.vars[var] * step + v
        return v

    def loop(self, n, body):
        me = self.n_loops
        self.n_loops += 1
        steps, tails = self.steps.get(me, ({}, {}))
        entry, before = dict(self.counts), dict(self.live)
        for s in self.counts:
            if steps.get(s):
                self.counts[s] = Count(entry[s].base, {**entry[s].steps, me: steps[s]})
        start = dict(self.counts)
        for key, tail in tails.items():
            rel, out = {}, []
            for sem, value in before.get(key, []):
                if value.same_steps(entry[sem]):
                    rel[sem] = max(rel.get(sem, -10**9), value.base - entry[sem].base)
                else:
                    out.append((sem, value))
            for sem, r in tail:
                rel[sem] = max(rel.get(sem, -10**9), r - steps.get(sem, 0))
            self.live[key] = out + [(sem, start[sem].plus(r)) for sem, r in rel.items()]
        started = dict(self.live)
        with self.nc.Fori(0, n) as it:
            self.vars[me] = it
            body()
        for lane in self.lanes:
            lane.seen = {}
        found = {s: self.counts[s].base - entry[s].base for s in self.counts}
        tails = {key: [(sem, v.base - entry[sem].base) for sem, v in toks if v.same_steps(start[sem])]
                 for key, toks in self.live.items() if toks is not started.get(key)}
        self.steps[me] = (found, tails)
        for s in self.counts:
            self.counts[s] = Count(entry[s].base + n * found[s], entry[s].steps)
        for key in tails:
            self.live[key] = [(sem, Count(v.base + (n - 1) * found[sem], entry[sem].steps)
                               if v.same_steps(start[sem]) else v) for sem, v in self.live[key]]


def build_program(nc, steps, weights, small, const, layer_par, gates, pool_mat, scale_row, x_in, mem1, mem2, pos, out):
    with ExitStack() as ctx:
        def sb(name, shape, dt=F32):
            return ctx.enter_context(nc.sbuf_tensor(name, shape, dt))

        names = ["act", "dve", "pe", "pool", "d_x", "d_mem", "d_small", "d_const", "d_gates", "d_pos", "d_par",
                 "d_pool", "d_mem2", "d_out"] + [f"d_w{i}" for i in range(SLOTS)]
        prog = Program(nc, {n: ctx.enter_context(nc.semaphore(n)) for n in names}, steps)
        A, V, T, G, SP = (Lane(prog, n, e) for n, e in (("act", nc.scalar), ("dve", nc.vector), ("pe", nc.tensor),
                                                        ("pool", nc.gpsimd), ("sp", nc.sync)))
        prog.lanes = [A, V, T, G, SP]
        live = prog.live

        raw = sb("raw", [P, SLOTS, UNIT])
        w_hi = sb("w_hi", [P, SLOTS, UNIT], F32R)
        w_lo = sb("w_lo", [P, SLOTS, UNIT], F32R)
        x = sb("x", [P, NT, D])
        xT = sb("xT", [P, KC, 2, S], F32R)
        memT = sb("memT", [P, KC, 2, S], F32R)
        hT = sb("hT", [P, 3, 2, 2, S], F32R)
        arena = sb("arena", [P, 16, 1024])
        par = sb("par", [P, N_LAYER])
        sm = sb("sm", [P, N_SMALL])
        cst = sb("cst", [P, N_CONST])
        stat = sb("stat", [P, 96])
        mhalf = sb("mhalf", [P, 12])
        rg = sb("rg", [P, 8, 4])
        trig = sb("trig", [P, 2, NT, 32])
        ps = ctx.enter_context(nc.psum_tensor("ps", [P, 8, 512], F32))

        def c(name):
            return cst[:, CONST[name]]

        def slot2(a):
            return arena[:, a:a + 2, :]

        ident = c("ident")

        def last_of(key):
            return live.get(key, [])

        class Stream:
            seq, taken, plan = 0, 0, []

        st = Stream()

        def prefetch():
            s = st.seq % SLOTS
            st.seq += 1
            width = st.plan.pop(0) if st.plan else UNIT
            nr = prog.value(prog.counts["unit"])
            prog.counts["unit"] = prog.counts["unit"].plus(1)
            src = weights[bass.ds(nc.sync.snap(nr), 1), :, 0:width].rearrange("a p n -> (a p) n") \
                if prog.counts["unit"].steps else weights[nr, :, 0:width]
            SP.after(*last_of(("raw", s)))
            loaded = SP.did(nc.sync.dma_start(raw[:, s, 0:width], src), f"d_w{s}", 16)
            A.after(loaded, *last_of(("slot", s)))
            hi = A.did(nc.scalar.activation(w_hi[:, s, 0:width], raw[:, s, 0:width], ACT.Copy))
            V.after(hi)
            lo = V.did(nc.vector.tensor_tensor(w_lo[:, s, 0:width], raw[:, s, 0:width],
                                               w_hi[:, s, 0:width].bitcast(F32), ALU.subtract))
            live["raw", s] = [lo]
            live["unit", s] = [lo]

        def take():
            s = st.taken % SLOTS
            st.taken += 1
            T.after(*live["unit", s])
            return s

        def release(s, last):
            tok = T.did(last)
            live["slot", s] = [tok]
            prefetch()
            return tok

        def plan(widths):
            assert not st.plan and all(w == UNIT for w in widths[:AHEAD])
            st.plan = list(widths[AHEAD:])

        def cols_tile(bank, s, src, half, wait):
            T.after(*wait, *last_of(("bank", bank)))
            wv = [w[:, s, :].rearrange("p (k n) -> p k n", k=KC) for w in (w_hi, w_lo)]
            cs = slice(half * P, half * P + P)
            for k in range(KC):
                both = src[:, k, :, :].rearrange("p a t -> p (a t)")
                def hi():
                    return nc.tensor.matmul(ps[:, bank, :], wv[0][:, k, cs], both, start=(k == 0), stop=(k == KC - 1))
                def lo():
                    return nc.tensor.matmul(ps[:, bank, 0:S], wv[1][:, k, cs], src[:, k, 0, :], start=False, stop=False)
                if k == 0:
                    hi()
                    last = lo()
                else:
                    lo()
                    last = hi()
            return last

        def rows_tile(bank, t, s, at, n, lhs, first, last_k):
            for j, (h, l) in enumerate(lhs):
                cs = slice(at + j * st.pitch, at + j * st.pitch + n)
                ts = slice(t * P, t * P + P)
                nc.tensor.matmul(ps[:, bank, 0:n], h[:, ts], w_hi[:, s, cs], start=(first and j == 0), stop=False)
                nc.tensor.matmul(ps[:, bank, 0:n], h[:, ts], w_lo[:, s, cs], start=False, stop=False)
                last = nc.tensor.matmul(ps[:, bank, 0:n], l[:, ts], w_hi[:, s, cs], start=False,
                                        stop=(last_k and j == len(lhs) - 1))
            return last

        def chunk(src, k):
            return src[:, k, 0, :], src[:, k, 1, :]

        def rows_unit(base, lhs, halves, n, first, last_k, wait=()):
            s = take()
            T.after(*wait)
            st.pitch = halves * n
            for t in range(NT):
                for h in range(halves):
                    bank = base + halves * t + h
                    if first:
                        T.after(*last_of(("bank", bank)))
                    last = rows_tile(bank, t, s, h * n, n, lhs, first, last_k)
            return release(s, last)

        def project(base, src, halves, n, per_unit, wait):
            for k in range(0, KC, per_unit):
                tok = rows_unit(base, [chunk(src, k + j) for j in range(per_unit)], halves, n,
                                k == 0, k + per_unit == KC, wait)
            return tok

        def recip_root(dst, src, n, scale, after):
            V.after(*after)
            ms = V.did(nc.vector.tensor_scalar(dst, src, scale, EPS, ALU.mult, ALU.add))
            G.after(ms, half_ready)
            return G.did(nc.gpsimd.tensor_tensor(dst, dst, mhalf[:, 0:n], ALU.pow))

        def transpose_rows(rows, t, n_chunks, bank0, wait):
            toks = []
            for b in range(0, n_chunks, 4):
                bank = bank0 + b // 4
                T.after(*wait, *last_of(("bank", bank)), const_ready)
                for j in range(min(4, n_chunks - b)):
                    last = nc.tensor.transpose(ps[:, bank, j * P:j * P + P], rows[:, (b + j) * P:(b + j + 1) * P], ident)
                toks.append(T.did(last))
            return toks

        def split(dst_hi, dst_lo, src, wait):
            A.after(*wait)
            hi = A.did(nc.scalar.activation(dst_hi, src, ACT.Copy))
            V.after(hi, *wait)
            return V.did(nc.vector.tensor_tensor(dst_lo, src, dst_hi.bitcast(F32), ALU.subtract))

        def norm_to_cols(dst, src, gain, rows, junk, tmp, bank0, st0, wait, key, between=None):
            done, scaled = [], []
            for t in range(NT):
                A.after(*wait)
                ss = stat[:, st0 + t:st0 + t + 1]
                sq = A.did(nc.scalar.activation(junk, src[:, t, :], ACT.Square, accum_out=ss))
                wait = [*wait, sq]
                root = recip_root(ss, ss, 1, 1.0 / D, [sq])
                V.after(root)
                scaled.append(V.did(nc.vector.tensor_scalar(rows[:, t, :], src[:, t, :], ss, None, ALU.mult)))
            if between:
                between()
            if dst is None:
                return scaled
            for t in range(NT):
                toks = transpose_rows(rows[:, t, :], t, KC, bank0 + 2 * t, [scaled[t]])
                for b, tok in enumerate(toks):
                    ks = slice(4 * b, 4 * b + 4)
                    done.append(evac_cols(dst, ks, slice(t * P, t * P + P), bank0 + 2 * t + b, P, gain[:, ks],
                                          tmp[:, t, b * 512:b * 512 + 512], [tok], key))
            return done

        def evac_cols(dst, ks, ts, bank, n, gain, tmp, wait, key):
            m = 512 // n
            pv = ps[:, bank, :].rearrange("p (k n) -> p k n", k=m)
            tv = tmp.rearrange("p (k n) -> p k n", k=m)
            V.after(*wait, *last_of(key))
            g = V.did(nc.vector.tensor_tensor(tv, pv, gain.unsqueeze(2).broadcast_to([P, m, n]), ALU.mult))
            live["bank", bank] = [g]
            return split(dst[:, ks, 0, ts], dst[:, ks, 1, ts], tv, [g, *last_of(key)])

        def head_norm(dst, src, heads, width, st0, junk, wait, gain_row=None):
            def hv(ap):
                return ap.rearrange("p (h c) -> p h c", h=heads)
            A.after(*wait)
            sq = A.did(nc.scalar.activation(junk, src, ACT.Square))
            V.after(sq, *wait)
            ss = stat[:, st0:st0 + heads]
            su = V.did(nc.vector.tensor_reduce(ss, hv(junk), AX.X, ALU.add))
            root = recip_root(ss, ss, heads, 1.0 / width, [su])
            V.after(root)
            tok = V.did(nc.vector.tensor_tensor(hv(dst), hv(src), ss.unsqueeze(2).broadcast_to([P, heads, width]),
                                                ALU.mult))
            if gain_row is not None:
                V.after(tok)
                return V.did(nc.vector.tensor_tensor(dst, dst, gain_row, ALU.mult)), [sq, tok]
            return tok, [sq, tok]

        def rows_to_cols(dst, rows, n_chunks, gain, bank0, wait):
            out_toks = []
            for t in range(NT):
                toks = transpose_rows(rows[t], t, n_chunks, bank0, [wait[t]])
                for b, tok in enumerate(toks):
                    m = min(4, n_chunks - 4 * b)
                    pv = ps[:, bank0 + b, 0:m * P].rearrange("p (k n) -> p k n", k=m)
                    dv = dst[:, 4 * b:4 * b + m, t * P:t * P + P]
                    V.after(tok)
                    if gain is None:
                        g = V.did(nc.vector.tensor_copy(dv, pv))
                    else:
                        g = V.did(nc.vector.tensor_tensor(dv, pv, gain[:, 4 * b:4 * b + m].unsqueeze(2)
                                                          .broadcast_to([P, m, P]), ALU.mult))
                    live["bank", bank0 + b] = [g]
                    out_toks.append(g)
            return out_toks

        def attention(heads, scale, p_buf, pt_buf, s_buf, wait, st0, key):
            n_banks = 4
            scored, pend = {}, []

            def scores(i):
                hd, bank = heads[i], i % n_banks
                T.after(*wait, *last_of(("bank", bank)))
                for t in range(NT):
                    for j, (q, k) in enumerate(zip(hd["q"], hd["k"])):
                        last = nc.tensor.matmul(ps[:, bank, t * S:t * S + S], q[:, t * P:t * P + P], k,
                                                start=(j == 0), stop=(j == len(hd["q"]) - 1))
                scored[i] = T.did(last)

            def softmax(i):
                hd, bank, b = heads[i], i % n_banks, i % 2
                src = ps[:, bank, :].rearrange("p (t n) -> p t n", t=NT)
                pb = p_buf[:, b * 512:b * 512 + 512].rearrange("p (t n) -> p t n", t=NT)
                base = st0 + 8 * b
                mx, den, sk = stat[:, base:base + 2], stat[:, base + 2:base + 4], stat[:, base + 4:base + 6]
                tok = scored[i]
                if hd.get("neg") is not None:
                    sv = s_buf[:, b * 512:b * 512 + 512].rearrange("p (t n) -> p t n", t=NT)
                    V.after(tok, const_ready, *last_of((key, "s", b)))
                    tok = V.did(nc.vector.tensor_tensor(sv, src, hd["neg"].rearrange("p (t n) -> p t n", t=NT), ALU.add))
                    live["bank", bank] = [tok]
                    src = sv
                V.after(tok, *last_of((key, "st", b)))
                m = V.did(nc.vector.tensor_reduce(mx, src, AX.X, ALU.max))
                V.after(m)
                if hd.get("sink") is not None:
                    m = V.did(nc.vector.tensor_scalar(mx, mx, scale, hd["sink"], ALU.mult, ALU.max))
                    V.after(m)
                    m = V.did(nc.vector.tensor_scalar(mx, mx, -1.0, None, ALU.mult))
                    A.after(m)
                    for t in range(NT):
                        sink_e = A.did(nc.scalar.activation(sk[:, t:t + 1], hd["sink"], ACT.Exp, bias=mx[:, t:t + 1]))
                else:
                    m = V.did(nc.vector.tensor_scalar(mx, mx, -scale, None, ALU.mult))
                A.after(m, *last_of((key, "p", b)))
                for t in range(NT):
                    e = A.did(nc.scalar.activation(pb[:, t, :], src[:, t, :], ACT.Exp, bias=mx[:, t:t + 1], scale=scale,
                                                   accum_out=den[:, t:t + 1]))
                if hd.get("neg") is None:
                    live["bank", bank] = [e]
                else:
                    live[key, "s", b] = [e]
                V.after(e)
                if hd.get("cnt") is not None:
                    cv = hd["cnt"].rearrange("p (t n) -> p t n", t=NT)
                    e = V.did(nc.vector.tensor_tensor(pb, pb, cv, ALU.mult))
                    V.after(e)
                    e = V.did(nc.vector.tensor_reduce(den, pb, AX.X, ALU.add))
                    V.after(e)
                if hd.get("sink") is not None:
                    V.after(sink_e)
                    e = V.did(nc.vector.tensor_tensor(den, den, sk, ALU.add))
                    V.after(e)
                r = V.did(nc.vector.reciprocal(den, den))
                V.after(r)
                pn = V.did(nc.vector.tensor_tensor(pb, pb, den.unsqueeze(2).broadcast_to([P, NT, S]), ALU.mult))
                live[key, "st", b] = [pn]
                return pb, pn

            def value(i, pb, pn):
                hd, b = heads[i], i % 2
                bank = 4 + b
                T.after(pn, const_ready, *last_of(("bank", bank)))
                for t in range(NT):
                    for mm in range(NT):
                        last = nc.tensor.transpose(ps[:, bank, mm * S + t * P:mm * S + t * P + P],
                                                   pb[:, t, mm * P:mm * P + P], ident)
                tr = T.did(last)
                live[key, "p", b] = [tr]
                ptb = pt_buf[:, b * 512:b * 512 + 512]
                A.after(tr, *last_of((key, "pt", b)))
                cp = A.did(nc.scalar.activation(ptb, ps[:, bank, :], ACT.Copy))
                live["bank", bank] = [cp]
                pend.append((i, ptb, cp))

            def product():
                i, ptb, cp = pend.pop(0)
                hd, b = heads[i], i % 2
                bank = 6 + hd["bank"]
                T.after(cp)
                if hd["open"]:
                    T.after(*last_of(("bank", bank)))
                for cc, (p0, p1, off) in enumerate(hd["place"]):
                    for mm in range(NT):
                        last = nc.tensor.matmul(ps[p0:p1, bank, off:off + S], hd["v"](mm, cc),
                                                ptb[:, mm * S:mm * S + S], start=(mm == 0), stop=(mm == NT - 1))
                pv = T.did(last)
                live[key, "pt", b] = [pv]
                if hd["close"] is not None:
                    ks, n = hd["close"]
                    src = ps[:, bank, 0:n * S].rearrange("p (k n) -> p k n", k=n)
                    tok = split(xT[:, ks, 0, :], xT[:, ks, 1, :], src, [pv, *last_of("xT")])
                    live["bank", bank] = [tok]
                    outs.append(tok)

            outs = []
            n = len(heads)
            for i in range(min(n_banks, n)):
                scores(i)
            for i in range(n):
                pb, pn = softmax(i)
                if i >= 1:
                    product()
                value(i, pb, pn)
                if i + n_banks < n:
                    scores(i + n_banks)
            product()
            return outs

        def add_rows(factor, after):
            toks = []
            for t in range(NT):
                for h in range(2):
                    bank, xs = 4 + 2 * t + h, x[:, t, h * 512:h * 512 + 512]
                    V.after(*after, *last_of("x"))
                    if factor == 1.0:
                        tok = V.did(nc.vector.tensor_tensor(xs, ps[:, bank, :], xs, ALU.add))
                    else:
                        tok = V.did(nc.vector.scalar_tensor_tensor(xs, ps[:, bank, :], factor, xs, ALU.mult, ALU.add))
                    live["bank", bank] = [tok]
                    toks.append(tok)
            live["x"] = toks

        def sum_halves(dst, tmp, bank, wait, key):
            pv = ps[:, bank:bank + 2, :]
            A.after(*wait, *last_of(key))
            b = A.did(nc.scalar.activation(tmp, pv[:, :, S:2 * S], ACT.Copy))
            V.after(b, *wait, *last_of(key))
            tok = V.did(nc.vector.tensor_tensor(dst, pv[:, :, 0:S], tmp, ALU.add))
            live["bank", bank] = [tok]
            live["bank", bank + 1] = [tok]
            return tok

        def buf(a, j=0):
            return arena[:, a, 512 * j:512 * j + 512].rearrange("p (k n) -> p k n", k=2)

        def up_unit(bank, wait):
            s = take()
            for h in range(2):
                last = cols_tile(bank + h, s, xT, h, wait)
            return release(s, last)

        def up_relu2(hb, wait):
            tok = up_unit(0, wait)
            z = sum_halves(buf(1, 0), buf(0, 0), 0, [tok], "ff_z")
            V.after(z, *last_of("ff_h"))
            h = V.did(nc.vector.scalar_tensor_tensor(buf(2, 0), buf(1, 0), 0.0, buf(1, 0), ALU.max, ALU.mult))
            live["ff_z"] = [h]
            tok = split(hT[:, hb, :, 0, :], hT[:, hb, :, 1, :], buf(2, 0), [h, *last_of(("hT", hb))])
            live["ff_h"] = [tok]
            live["h", hb] = [tok]

        def up_swiglu(hb, wait):
            tok = up_unit(0, wait)
            g = sum_halves(buf(1, 0), buf(0, 0), 0, [tok], "ff_z")
            A.after(g, *last_of("ff_g"))
            sg = A.did(nc.scalar.activation(buf(2, 0), buf(1, 0), ACT.Sigmoid))
            V.after(sg, *last_of("ff_g"))
            gs = V.did(nc.vector.tensor_tensor(buf(3, 0), buf(1, 0), buf(2, 0), ALU.mult))
            live["ff_z"] = [gs]
            tok = up_unit(2, wait)
            u = sum_halves(buf(4, 0), buf(0, 1), 2, [tok], "ff_u")
            V.after(u, gs, *last_of("ff_h"))
            h = V.did(nc.vector.tensor_tensor(buf(5, 0), buf(3, 0), buf(4, 0), ALU.mult))
            live["ff_g"] = [h]
            live["ff_u"] = [h]
            tok = split(hT[:, hb, :, 0, :], hT[:, hb, :, 1, :], buf(5, 0), [h, *last_of(("hT", hb))])
            live["ff_h"] = [tok]
            live["h", hb] = [tok]

        def down(hb, last_k):
            tok = rows_unit(4, [(hT[:, hb, j, 0, :], hT[:, hb, j, 1, :]) for j in range(2)], 2, 512, False, last_k,
                            live["h", hb])
            live["hT", hb] = [tok]
            return tok

        def feed_forward(gain, wide, up, per_body, factor, par_tok=()):
            ready = norm_to_cols(xT, x, gain, slot2(6), arena[:, 8, :], slot2(10), 0, 0,
                                 [*last_of("x"), *par_tok], "xT")
            for b in range(4):
                T.after(*last_of(("bank", 4 + b)), zero_ready)
                nc.tensor.matmul(ps[:, 4 + b, :], zero[:, 0:P], zero[:, :], start=True, stop=False)
            up(0, ready)
            n = wide // FF - 1
            assert n % per_body == 0

            def body():
                for j in range(per_body):
                    up((j + 1) % per_body, ())
                    down(j, False)
            prog.loop(n // per_body, body)
            tok = down(0, True)
            live["xT"] = [tok]
            add_rows(factor, [tok])

        zero = sb("zero", [P, 512], mybir.dt.bfloat16)
        half_ready = G.did(nc.gpsimd.memset(mhalf[:, :], -0.5))
        zero_ready = G.did(nc.gpsimd.memset(zero[:, :], 0.0))

        x_ready = A.did(nc.scalar.dma_start(x[:, :, :], x_in.rearrange("(t p) d -> p t d", p=P)), "d_x", 16)
        live["x"] = [x_ready]
        mem_ready = A.did(nc.scalar.dma_start(slot2(4), mem1.rearrange("(t p) d -> p t d", p=P)), "d_mem", 16)
        const_ready = A.did(nc.scalar.dma_start(cst[:, :], const), "d_const", 16)
        small_ready = A.did(nc.scalar.dma_start(sm[:, :], small), "d_small", 16)
        gates_ready = A.did(nc.scalar.dma_start(par[:, 0:1024], gates), "d_gates", 16)
        pos_i = sb("pos_i", [P, NT], I32)
        pos_ready = A.did(nc.scalar.dma_start(pos_i[:, :], pos), "d_pos", 16)
        for _ in range(AHEAD):
            prefetch()

        def g1(name):
            return sm[:, SMALL[name]]

        ready = norm_to_cols(xT, x, g1("mix_g0"), slot2(6), arena[:, 8, :], slot2(10), 0, 0,
                             [x_ready, small_ready], "xT")
        XR = arena[:, 0:2, :].rearrange("p a n -> p (a n)")[:, 0:4 * 259].rearrange("p (c n) -> p c n", c=4)
        XC, R, I_, DEC, AA, GATE, GTMP, HS = (arena[:, a, :] for a in (2, 3, 12, 5, 14, 8, 9, 13))

        def quad(ap):
            return ap.rearrange("p (c n) -> p c n", c=4)

        V.after(*ready)
        V.did(nc.vector.memset(XR[:, :, 0:3], 0.0))
        pad_ready = ("dve", prog.counts["dve"])
        xr_toks = []
        for j in range(2):
            tok = up_unit(2 * j, ready)
            xr_toks.append(sum_halves(XR[:, 2 * j:2 * j + 2, 3:259], buf(15, 0), 2 * j, [tok], "sh"))
            live["sh"] = [xr_toks[-1]]

        mem_toks = norm_to_cols(memT, slot2(4), g1("mem_g"), slot2(6), arena[:, 8, :], slot2(10), 0, 2,
                                [mem_ready, *ready], "memT")

        lam, ab, ee, zz, z2, acc, neg = g1("lam"), *(rg[:, i, :] for i in range(6))
        V.after(small_ready)
        t0 = V.did(nc.vector.tensor_scalar(neg, lam, -1.0, None, ALU.mult))
        V.after(t0)
        t0 = V.did(nc.vector.tensor_tensor(ab, lam, neg, ALU.max))
        A.after(t0)
        t0 = A.did(nc.scalar.activation(ee, ab, ACT.Exp, scale=-1.0))
        V.after(t0)
        t0 = V.did(nc.vector.tensor_scalar(zz, ee, 2.0, None, ALU.add))
        V.after(t0)
        t0 = V.did(nc.vector.reciprocal(zz, zz))
        V.after(t0)
        t0 = V.did(nc.vector.tensor_tensor(zz, zz, ee, ALU.mult))
        V.after(t0)
        t0 = V.did(nc.vector.tensor_tensor(z2, zz, zz, ALU.mult))
        V.after(t0)
        t0 = V.did(nc.vector.tensor_scalar(acc, z2, 1.0 / 17, 1.0 / 15, ALU.mult, ALU.add))
        for odd in (13, 11, 9, 7, 5, 3, 1):
            V.after(t0)
            t0 = V.did(nc.vector.tensor_tensor(acc, acc, z2, ALU.mult))
            V.after(t0)
            t0 = V.did(nc.vector.tensor_scalar(acc, acc, 1.0 / odd, None, ALU.add))
        V.after(t0)
        t0 = V.did(nc.vector.tensor_tensor(acc, acc, zz, ALU.mult))
        V.after(t0)
        t0 = V.did(nc.vector.tensor_scalar(neg, neg, 0.0, None, ALU.max))
        V.after(t0)
        t0 = V.did(nc.vector.scalar_tensor_tensor(acc, acc, 2.0, neg, ALU.mult, ALU.add))
        V.after(t0)
        sp4 = rg[:, 6, :]
        decay_ready = V.did(nc.vector.tensor_scalar(sp4, acc, 4.0, None, ALU.mult))

        conv_toks = []
        for ch in range(4):
            xc = quad(XC)[:, ch, :]
            cw = g1("conv_w")
            V.after(*xr_toks, pad_ready)
            t0 = V.did(nc.vector.tensor_scalar(xc, XR[:, ch, 0:S], cw[:, ch:ch + 1], g1("conv_b")[:, ch:ch + 1],
                                               ALU.mult, ALU.add))
            for j in range(1, 4):
                V.after(t0)
                t0 = V.did(nc.vector.scalar_tensor_tensor(xc, XR[:, ch, j:j + S], cw[:, 4 * j + ch:4 * j + ch + 1], xc,
                                                          ALU.mult, ALU.add))
            conv_toks.append(t0)
        gate_toks = []
        for j in range(2):
            tok = up_unit(2 * j, ready)
            gate_toks.append(sum_halves(quad(GATE)[:, 2 * j:2 * j + 2, :], buf(15, 0), 2 * j, [tok], "sh"))
            live["sh"] = [gate_toks[-1]]
        gw = par[:, 0:1024].rearrange("p (g n) -> p g n", g=8)
        sig = []
        for g, (dst, bias) in enumerate(((R, "ga_b"), (I_, "gx_b"))):
            for ch in range(4):
                bank = 2 * g + ch // 2
                T.after(*conv_toks, gates_ready, *last_of(("bank", bank)))
                last = nc.tensor.matmul(ps[:, bank, (ch % 2) * S:(ch % 2) * S + S], gw[:, 4 * g + ch, :],
                                        quad(XC)[:, ch, :], start=True, stop=True)
                if ch % 2:
                    tok = T.did(last)
                    A.after(tok, small_ready, *gate_toks)
                    for c2 in (ch - 1, ch):
                        s_ = A.did(nc.scalar.activation(quad(dst)[:, c2, :], ps[:, bank, (c2 % 2) * S:(c2 % 2) * S + S],
                                                        ACT.Sigmoid, bias=g1(bias)[:, c2:c2 + 1]))
                    live["bank", bank] = [s_]
                    sig.append(s_)

        A.after(decay_ready, *sig)
        for ch in range(4):
            th = A.did(nc.scalar.activation(quad(R)[:, ch, :], quad(R)[:, ch, :], ACT.Tanh, scale=sp4[:, ch:ch + 1]))
        V.after(th)
        t0 = V.did(nc.vector.tensor_scalar(DEC, R, 1.0, None, ALU.add))
        V.after(t0)
        t0 = V.did(nc.vector.reciprocal(DEC, DEC))
        V.after(t0)
        t0 = V.did(nc.vector.scalar_tensor_tensor(R, R, 2.0, DEC, ALU.mult, ALU.mult))
        V.after(t0)
        a_tok = V.did(nc.vector.tensor_scalar(AA, R, -1.0, 1.0, ALU.mult, ALU.add))
        V.after(a_tok)
        t0 = V.did(nc.vector.scalar_tensor_tensor(R, AA, 1.0, R, ALU.add, ALU.mult))
        A.after(*gate_toks)
        g2 = A.did(nc.scalar.activation(GTMP, GATE, ACT.Square))
        V.after(g2)
        t1 = V.did(nc.vector.tensor_scalar(GTMP, GTMP, 0.044715, 1.0, ALU.mult, ALU.add))
        V.after(t1)
        t1 = V.did(nc.vector.tensor_tensor(GTMP, GTMP, GATE, ALU.mult))
        A.after(t1)
        t1 = A.did(nc.scalar.activation(GTMP, GTMP, ACT.Tanh, scale=float(np.sqrt(2 / np.pi))))
        A.after(t0)
        root = A.did(nc.scalar.activation(R, R, ACT.Sqrt))
        V.after(t1)
        gelu_tok = V.did(nc.vector.scalar_tensor_tensor(GATE, GTMP, 1.0, GATE, ALU.add, ALU.mult))
        V.after(*sig, *conv_toks)
        t0 = V.did(nc.vector.tensor_tensor(I_, I_, XC, ALU.mult))
        V.after(t0, root)
        t0 = V.did(nc.vector.tensor_tensor(I_, I_, R, ALU.mult))
        V.after(t0)
        for ch in range(4):
            t0 = V.did(nc.vector.tensor_tensor_scan(quad(HS)[:, ch, :], quad(AA)[:, ch, :], quad(I_)[:, ch, :], 0.0,
                                                    ALU.mult, ALU.add))
        V.after(t0, gelu_tok)
        yb_tok = V.did(nc.vector.scalar_tensor_tensor(GATE, HS, 0.5, GATE, ALU.mult, ALU.mult))

        qk_tok = project(4, xT, 2, 512, 2, ready)
        ROWS, KT, QT, VB = slot2(0), quad(arena[:, 4, :]), quad(arena[:, 6, :]), arena[:, 7, :]
        v_tok = project(0, xT, 1, 512, 4, ready)
        live["xT"] = [v_tok]
        rows_tok = []
        for t in range(NT):
            src = ps[:, 4 + 2 * t:6 + 2 * t, :].rearrange("p a n -> p (a n)")
            tok, banks = head_norm(ROWS[:, t, :], src, 8, P, 16 + 8 * t, arena[:, 15, :], [qk_tok, *conv_toks, *last_of("junk")])
            live["junk"] = banks
            live["bank", 4 + 2 * t] = live["bank", 5 + 2 * t] = banks
            rows_tok.append(tok)
        for t in range(NT):
            A.after(v_tok)
            vt = A.did(nc.scalar.activation(VB[:, t * 512:t * 512 + 512], ps[:, t, :], ACT.Copy))
            live["bank", t] = [vt]
        q_tok = rows_to_cols(QT, [ROWS[:, t, 0:512] for t in range(NT)], 4, g1("ev_q"), 2, rows_tok)
        k_tok = rows_to_cols(KT, [ROWS[:, t, 512:1024] for t in range(NT)], 4, g1("ev_k"), 3, rows_tok)
        heads = [dict(q=[QT[:, h, :]], k=[KT[:, h, :]], neg=c("neg1"), cnt=c("cnt"),
                      v=lambda mm, cc, h=h: VB[:, mm * 512 + h * P:mm * 512 + h * P + P],
                      place=[(0, P, (h % 2) * S)], bank=h // 2, open=(h % 2 == 0),
                      close=(slice(h - 1, h + 1), 2) if h % 2 else None) for h in range(4)]
        o_toks = attention(heads, P ** -0.5, arena[:, 10, :], arena[:, 11, :], arena[:, 15, :],
                           [*q_tok, *k_tok, vt], 40, "at0")
        y_tok = split(xT[:, 4:8, 0, :], xT[:, 4:8, 1, :], quad(GATE), [yb_tok, v_tok])
        tok = project(4, xT, 2, 512, 2, [*o_toks, y_tok])
        live["xT"] = [tok]
        add_rows(1.0, [tok])

        def cross_attention(layer):
            xk = project(4, memT, 2, 512, 2, mem_toks)
            KR, KTX, QTX, VX = slot2(10), slot2(0), slot2(2), slot2(4)
            KT8, QT8 = (b.rearrange("p a n -> p (a n)").rearrange("p (k n) -> p k n", k=8) for b in (KTX, QTX))
            k_rows = []
            for t in range(NT):
                src = ps[:, 4 + 2 * t:6 + 2 * t, :].rearrange("p a n -> p (a n)")
                tok, banks = head_norm(KR[:, t, :], src, 4, 256, 16 + 4 * t, arena[:, 9, :],
                                       [xk, *last_of("x"), *last_of("junk")])
                live["junk"] = banks
                live["bank", 4 + 2 * t] = live["bank", 5 + 2 * t] = banks
                k_rows.append(tok)
            x_cols = norm_to_cols(xT, x, g1(f"xat_g{layer}"), slot2(6), arena[:, 8, :], slot2(12), 0, 0,
                                  [*last_of("x")], "xT")
            xq = project(0, xT, 2, 512, 2, x_cols)
            live["xT"] = [xq]
            k_cols = rows_to_cols(KT8, [KR[:, t, :] for t in range(NT)], 8, None, 4, k_rows)
            xv = project(4, memT, 2, 512, 2, ())
            q_rows = []
            for t in range(NT):
                src = ps[:, 2 * t:2 * t + 2, :].rearrange("p a n -> p (a n)")
                tok, banks = head_norm(slot2(6)[:, t, :], src, 4, 256, 24 + 4 * t, arena[:, 9, :],
                                       [xq, *x_cols, *last_of("junk")])
                live["junk"] = banks
                live["bank", 2 * t] = live["bank", 2 * t + 1] = banks
                q_rows.append(tok)
            q_cols = rows_to_cols(QT8, [slot2(6)[:, t, :] for t in range(NT)], 8, None, 0, q_rows)
            gains = []
            for dst, name, toks in ((KT8, "xk", k_cols), (QT8, "xq", q_cols)):
                dv = dst.rearrange("p (h c) n -> p h c n", c=2)
                V.after(*toks)
                for cc in range(2):
                    gains.append(V.did(nc.vector.tensor_scalar(dv[:, :, cc, :], dv[:, :, cc, :],
                                                               g1(f"{name}{layer}")[:, cc:cc + 1], None, ALU.mult)))
            A.after(xv, *last_of("x"))
            for t in range(NT):
                src = ps[:, 4 + 2 * t:6 + 2 * t, :].rearrange("p a n -> p (a n)")
                vv = A.did(nc.scalar.activation(VX[:, t, :], src, ACT.Copy))
                live["bank", 4 + 2 * t] = live["bank", 5 + 2 * t] = [vv]
            heads = [dict(q=[QT8[:, 2 * h + cc, :] for cc in range(2)], k=[KT8[:, 2 * h + cc, :] for cc in range(2)],
                          v=lambda mm, cc, h=h: VX[:, mm, h * 256 + cc * P:h * 256 + cc * P + P],
                          place=[(0, P, 0), (0, P, S)], bank=h % 2, open=True,
                          close=(slice(2 * h, 2 * h + 2), 2)) for h in range(4)]
            o = attention(heads, 256 ** -0.5, arena[:, 12, :], arena[:, 13, :], arena[:, 14, :], [*gains, vv], 40, "xa")
            tok = project(4, xT, 2, 512, 2, o)
            live["xT"] = [tok]
            live["memT"] = [xv]
            add_rows(1.0, [tok])

        cross_attention(0)
        feed_forward(g1("mlp_g0"), D_FF, up_relu2, 3, 1.0)

        AM = slot2(4).rearrange("p a n -> p (a n)").rearrange("p (s g n) -> p s g n", s=2, g=4)
        A.after(*last_of("x"))
        pool_ready = A.did(nc.scalar.dma_start(slot2(4), pool_mat.rearrange("p (a n) -> p a n", a=2)), "d_pool", 16)
        pool_ready = A.did(nc.scalar.dma_start(arena[:, 14, :], scale_row), "d_pool", 16)
        rows_ready = norm_to_cols(None, x, None, slot2(6), arena[:, 8, :], None, 0, 0, [*last_of("x")], None)
        d_toks = []
        for kc in range(KC):
            bank, off, g = kc // 2, (kc % 2) * S, kc // 2
            T.after(pool_ready, *rows_ready, *last_of(("bank", bank)))
            nc.tensor.matmul(ps[:, bank, off:off + S], slot2(6)[:, 0, kc * P:kc * P + P], AM[:, 0, g, :], start=True,
                             stop=False)
            last = nc.tensor.matmul(ps[:, bank, off + P:off + S], slot2(6)[:, 1, kc * P:kc * P + P], AM[:, 1, g, P:S],
                                    start=False, stop=True)
            if kc % 2:
                tok = T.did(last)
                d_toks.append(evac_cols(xT, slice(kc - 1, kc + 1), slice(0, S), bank, S, g1("mix_g1")[:, kc - 1:kc + 1],
                                        slot2(10)[:, bank // 2, (bank % 2) * 512:(bank % 2) * 512 + 512], [tok], "xT"))
        s = take()
        for g in range(4):
            for t in range(NT):
                bank, off = 4 + 2 * t + g // 2, (g % 2) * S
                T.after(*d_toks, *last_of(("bank", bank)))
                for j in range(2):
                    h, l = chunk(xT, 2 * g + j)
                    cs, ts = slice((2 * g + j) * S, (2 * g + j) * S + S), slice(t * P, t * P + P)
                    o = ps[:, bank, off:off + S]
                    nc.tensor.matmul(o, h[:, ts], w_hi[:, s, cs], start=(j == 0), stop=False)
                    nc.tensor.matmul(o, h[:, ts], w_lo[:, s, cs], start=False, stop=False)
                    last = nc.tensor.matmul(o, l[:, ts], w_hi[:, s, cs], start=False, stop=(j == 1))
        tok = release(s, last)
        live["xT"] = [tok]
        toks = []
        for t in range(NT):
            for h in range(2):
                bank, tmp = 4 + 2 * t + h, slot2(12)[:, t, h * 512:h * 512 + 512]
                V.after(tok)
                m_ = V.did(nc.vector.tensor_tensor(tmp, ps[:, bank, :], arena[:, 14, h * 512:h * 512 + 512], ALU.mult))
                live["bank", bank] = [m_]
                xs = x[:, t, h * 512:h * 512 + 512]
                V.after(m_, *rows_ready)
                toks.append(V.did(nc.vector.tensor_tensor(xs, xs, tmp, ALU.add)))
        live["x"] = toks

        cross_attention(1)
        feed_forward(g1("mlp_g1"), D_FF, up_relu2, 3, 1.0)

        MAGIC = 1.5 * 2.0 ** 23
        C1 = 6.28125
        C2 = float(np.float32(2 * np.pi - C1))
        C2 = float(np.float32(np.round(C2 * 2 ** 21) / 2 ** 21))
        C3 = float(2 * np.pi - C1 - C2)
        posf, ang, kk, red = stat[:, 80:82], arena[:, 0, 0:64], arena[:, 0, 64:128], arena[:, 0, 128:192]
        V.after(pos_ready, *last_of("x"))
        t0 = V.did(nc.vector.tensor_copy(posf, pos_i[:, :]))
        V.after(t0, const_ready)
        for t in range(NT):
            t0 = V.did(nc.vector.tensor_scalar(ang[:, 32 * t:32 * t + 32], c("freq"), posf[:, t:t + 1], None, ALU.mult))
        for i, (shift, phase) in enumerate(((0.25, np.pi / 2), (0.0, 0.0))):
            V.after(t0)
            t0 = V.did(nc.vector.tensor_scalar(kk, ang, float(1 / (2 * np.pi)), shift, ALU.mult, ALU.add))
            V.after(t0)
            t0 = V.did(nc.vector.tensor_scalar(kk, kk, MAGIC, None, ALU.add))
            V.after(t0)
            t0 = V.did(nc.vector.tensor_scalar(kk, kk, -MAGIC, None, ALU.add))
            V.after(t0)
            t0 = V.did(nc.vector.scalar_tensor_tensor(red, kk, -C1, ang, ALU.mult, ALU.add))
            for cc in (C2, C3):
                V.after(t0)
                t0 = V.did(nc.vector.scalar_tensor_tensor(red, kk, -cc, red, ALU.mult, ALU.add))
            V.after(t0)
            t0 = V.did(nc.vector.tensor_scalar(red, red, float(phase), float(np.float32(3.1415925)), ALU.add, ALU.min))
            V.after(t0)
            t0 = V.did(nc.vector.tensor_scalar(red, red, -3.1415925, None, ALU.max))
            A.after(t0)
            t0 = A.did(nc.scalar.activation(trig[:, i, :, :].rearrange("p a n -> p (a n)"), red, ACT.Sin))
        trig_ready = t0
        live["rope"] = [t0]

        def lp(name, n=None):
            return par[:, LAYER[name]]

        def layer():
            lid = prog.n_loops - 1
            which = nc.scalar.snap(prog.vars[lid] + 0)
            A.after(*last_of("x"), *last_of("par"), *last_of("rope"))
            par_ready = A.did(nc.scalar.dma_start(par[:, :], layer_par[bass.ds(which, 1), :, :]
                                                  .rearrange("a p n -> (a p) n")), "d_par", 16)
            par_tok = [par_ready]
            feed_forward(lp("ffn1_g"), D_FF2, up_swiglu, 2, 0.5, par_tok)

            MR = slot2(2)
            A.after(*last_of("x"))
            mem_in = A.did(nc.scalar.dma_start(MR, mem2.rearrange("(t p) d -> p t d", p=P)), "d_mem2", 16)
            x_cols = norm_to_cols(xT, x, lp("mix_g"), slot2(0), arena[:, 15, :], slot2(6), 0, 0, [*last_of("x")], "xT")
            Z6 = arena[:, 9:11, :].rearrange("p a n -> p (a n)")[:, 0:1536].rearrange("p (k n) -> p k n", k=6)
            YP = arena[:, 11, 0:3 * 286].rearrange("p (k n) -> p k n", k=3)
            YC = arena[:, 12, 0:768].rearrange("p (k n) -> p k n", k=3)
            plan([UNIT] * 5 + [PARTIAL] * 4 + [UNIT] * 6)
            V.after(*last_of("x"))
            pad = V.did(nc.vector.memset(YP[:, :, 0:30], 0.0))
            zt = []
            for j in range(3):
                tok = up_unit(2 * (j % 2), x_cols)
                zt.append(sum_halves(Z6[:, 2 * j:2 * j + 2, :], buf(5, 0), 2 * (j % 2), [tok], "sh"))
                live["sh"] = [zt[-1]]
            A.after(*zt)
            sg = A.did(nc.scalar.activation(Z6[:, 3:6, :], Z6[:, 3:6, :], ACT.Sigmoid))
            V.after(sg, *zt, pad)
            glu = V.did(nc.vector.tensor_tensor(YP[:, :, 30:286], Z6[:, 0:3, :], Z6[:, 3:6, :], ALU.mult))

            cw, taps = lp("conv_w"), []
            conv_last = [None, None, None]

            def tap(j, ch):
                if j == 0:
                    V.after(glu, *par_tok)
                    conv_last[ch] = V.did(nc.vector.tensor_scalar(YC[:, ch, :], YP[:, ch, 0:S], cw[:, ch:ch + 1],
                                                                  lp("conv_b")[:, ch:ch + 1], ALU.mult, ALU.add))
                else:
                    V.after(conv_last[ch])
                    conv_last[ch] = V.did(nc.vector.scalar_tensor_tensor(
                        YC[:, ch, :], YP[:, ch, j:j + S], cw[:, 3 * j + ch:3 * j + ch + 1], YC[:, ch, :],
                        ALU.mult, ALU.add))
            taps = [(j, ch) for j in range(31) for ch in range(3)]

            def run_taps(n):
                for _ in range(min(n, len(taps))):
                    tap(*taps.pop(0))

            for k in range(0, KC, 4):
                qk_tok = rows_unit(4, [chunk(xT, k + j) for j in range(4)], 1, 512, k == 0, k == 4, x_cols)
                run_taps(10)
            for k in range(0, KC, 2):
                mv_tok = rows_unit(6, [chunk(xT, k + j) for j in range(2)], 1, 384, k == 0, k == 6, x_cols)
                run_taps(4)
            live["xT"] = [mv_tok]
            m_cols = norm_to_cols(memT, MR, lp("mem_g"), slot2(6), arena[:, 15, :], slot2(13), 0, 2,
                                  [mem_in, *last_of(("bank", 3)), *x_cols], "memT")
            QR = slot2(0)
            VW = arena[:, 4, 0:256].rearrange("p (t n) -> p t n", t=NT)
            MV = arena[:, 4, 256:768].rearrange("p (t n) -> p t n", t=NT)
            rows_t = []
            cosb, sinb = (trig[:, i, :, :].unsqueeze(2).broadcast_to([P, NT, 8, 32]) for i in range(2))
            for t in range(NT):
                tok, banks = head_norm(QR[:, t, 0:512], ps[:, 4 + t, :], 8, 64, 16 + 12 * t, arena[:, 15, 0:512],
                                       [qk_tok, *x_cols, *last_of("junk"), *par_tok, *m_cols], lp("qk_g"))
                live["junk"] = live["bank", 4 + t] = banks
                tok2, banks = head_norm(QR[:, t, 512:768], ps[:, 6 + t, 0:256], 4, 64, 24 + 12 * t,
                                        arena[:, 15, 512:768], [mv_tok, *last_of("junk")])
                live["junk"] = [*live["junk"], *banks]
                A.after(mv_tok, *last_of("x"), *banks)
                vt = A.did(nc.scalar.activation(VW[:, t, :], ps[:, 6 + t, 256:384], ACT.Copy))
                live["bank", 6 + t] = [*banks, vt]
                rows_t.append([tok, tok2])
            m_tok = project(0, memT, 1, 512, 4, m_cols)
            live["memT"] = [m_tok]
            qv = QR[:, :, 0:512].rearrange("p t (h c) -> p t h c", c=64)
            x1, x2 = qv[:, :, :, 0:32], qv[:, :, :, 32:64]
            r1, r2, r3 = (a.rearrange("p (t h c) -> p t h c", t=NT, c=32)
                          for a in (arena[:, 13, 0:512], arena[:, 13, 512:1024], arena[:, 14, 0:512]))
            V.after(*rows_t[0], *rows_t[1], trig_ready)
            r = [V.did(nc.vector.tensor_tensor(r1, x1, sinb, ALU.mult))]
            r.append(V.did(nc.vector.tensor_tensor(r2, x2, sinb, ALU.mult)))
            V.after(*r)
            r = [V.did(nc.vector.tensor_tensor(r3, x1, cosb, ALU.mult))]
            r.append(V.did(nc.vector.tensor_tensor(x2, x2, cosb, ALU.mult)))
            V.after(*r)
            r = [V.did(nc.vector.tensor_tensor(x1, r3, r2, ALU.subtract)),
                 V.did(nc.vector.tensor_tensor(x2, x2, r1, ALU.add))]
            QKT = slot2(2).rearrange("p a n -> p (a n)")[:, 0:1536].rearrange("p (k n) -> p k n", k=6)
            MKT = arena[:, 5, 0:512].rearrange("p (k n) -> p k n", k=2)
            MKR = arena[:, 5, 512:1024].rearrange("p (t n) -> p t n", t=NT)
            qk_cols = rows_to_cols(QKT, [QR[:, t, 0:768] for t in range(NT)], 6, None, 2, [r[-1], r[-1]])
            V.after(*qk_cols)
            for j in range(2):
                mq = V.did(nc.vector.tensor_scalar(QKT[:, 4 + j, :], QKT[:, 4 + j, :], lp("mq_g")[:, j:j + 1], None, ALU.mult))
            mk_rows = []
            for t in range(NT):
                tok, banks = head_norm(MKR[:, t, :], ps[:, t, 0:256], 4, 64, 60 + 4 * t, arena[:, 15, 0:256],
                                       [m_tok, *zt, *last_of("junk")])
                live["junk"] = banks
                A.after(m_tok, *banks)
                vt = A.did(nc.scalar.activation(MV[:, t, :], ps[:, t, 256:512], ACT.Copy))
                live["bank", t] = [*banks, vt]
                mk_rows.append(tok)
            mk_cols = rows_to_cols(MKT, [MKR[:, t, :] for t in range(NT)], 2, lp("mk_g"), 2, mk_rows)

            heads = []
            for j in range(3):
                for side in range(2):
                    ss = slice(64 * side, 64 * side + 64)
                    heads.append(dict(q=[QKT[ss, j, :]], k=[QKT[ss, 3, :]], neg=c("neg2"),
                                      sink=lp("sinks")[:, 2 * j + side:2 * j + side + 1],
                                      v=lambda mm, cc, ss=ss: VW[:, mm, ss], place=[(64 * side, 64 * side + 64, 0)],
                                      bank=j % 2, open=(side == 0), close=(slice(3 + j, 4 + j), 1) if side else None))
            for j in range(2):
                for side in range(2):
                    ss = slice(64 * side, 64 * side + 64)
                    vs = slice(128 * j + 64 * side, 128 * j + 64 * side + 64)
                    heads.append(dict(q=[QKT[ss, 4 + j, :]], k=[MKT[ss, j, :]],
                                      v=lambda mm, cc, vs=vs: MV[:, mm, vs], place=[(64 * side, 64 * side + 64, 0)],
                                      bank=(j + 1) % 2, open=(side == 0),
                                      close=(slice(6 + j, 7 + j), 1) if side else None))
            o = attention(heads, 64 ** -0.5, arena[:, 6, :], arena[:, 7, :], arena[:, 8, :],
                          [*qk_cols, mq, *mk_cols, vt], 40, "sw")
            run_taps(93)

            MU, LT, VR = arena[:, 13, 0:256], arena[:, 14, 0:768].rearrange("p (k n) -> p k n", k=3), arena[:, 13, 256:512]

            def channel_sum(src, after):
                T.after(*after, *last_of(("bank", 0)))
                for k in range(3):
                    last = nc.tensor.matmul(ps[:, 0, 0:S], c("ones"), src[:, k, :], start=(k == 0), stop=(k == 2))
                return T.did(last)
            tok = channel_sum(YC, conv_last)
            A.after(tok, *r)
            t0 = A.did(nc.scalar.activation(MU, ps[:, 0, 0:S], ACT.Copy, scale=1.0 / 384))
            live["bank", 0] = [t0]
            V.after(t0)
            t0 = V.did(nc.vector.tensor_tensor(YC, YC, MU.unsqueeze(1).broadcast_to([P, 3, S]), ALU.subtract))
            A.after(t0)
            sq = A.did(nc.scalar.activation(LT, YC, ACT.Square))
            tok = channel_sum(LT, [sq])
            V.after(tok)
            t1 = V.did(nc.vector.tensor_scalar(VR, ps[:, 0, 0:S], 1.0 / 384, EPS, ALU.mult, ALU.add))
            live["bank", 0] = [t1]
            V.after(t1)
            t1 = V.did(nc.vector.reciprocal(VR, VR))
            A.after(t1)
            t1 = A.did(nc.scalar.activation(VR, VR, ACT.Sqrt))
            V.after(t1)
            t1 = V.did(nc.vector.tensor_tensor(YC, YC, VR.unsqueeze(1).broadcast_to([P, 3, S]), ALU.mult))
            V.after(t1)
            for k in range(3):
                t1 = V.did(nc.vector.tensor_scalar(YC[:, k, :], YC[:, k, :], lp("ln_g")[:, k:k + 1],
                                                   lp("ln_b")[:, k:k + 1], ALU.mult, ALU.add))
            A.after(t1)
            t2 = A.did(nc.scalar.activation(LT, YC, ACT.Sigmoid))
            V.after(t2)
            t2 = V.did(nc.vector.tensor_tensor(YC, YC, LT, ALU.mult))
            y_tok = split(xT[:, 0:3, 0, :], xT[:, 0:3, 1, :], YC, [t2, mv_tok])
            tok = project(4, xT, 2, 512, 2, [*o, y_tok])
            live["xT"] = [tok]
            add_rows(1.0, [tok])

            feed_forward(lp("ffn2_g"), D_FF2, up_swiglu, 2, 0.5, par_tok)

            toks = norm_to_cols(None, x, None, slot2(6), arena[:, 8, :], None, 0, 0, [*last_of("x")], None)
            xo = []
            for t in range(NT):
                V.after(*toks)
                xo.append(V.did(nc.vector.tensor_tensor(x[:, t, :], slot2(6)[:, t, :], lp("final_g"), ALU.mult)))
            live["x"] = xo
            live["par"] = xo

        live["par"] = [gates_ready, ("pe", prog.counts["pe"])]
        prog.loop(2, layer)

        SP.after(*last_of("x"))
        done = SP.did(nc.sync.dma_start(out.rearrange("(t p) d -> p t d", p=P), x[:, :, :]), "d_out", 16)
        SP.after(done)


def _up_units(w):
    n = w.shape[1] // 256
    return w.reshape(KC, P, n, 256).transpose(2, 1, 0, 3).reshape(n, P, UNIT)


def _down_units(w, cols=1024):
    j = UNIT // cols
    n = w.shape[0] // (P * j)
    return w.reshape(n, j, P, cols).transpose(0, 2, 1, 3).reshape(n, P, UNIT)


def _narrow_units(w):
    u = np.zeros((4, P, UNIT), w.dtype)
    u[:, :, 0:PARTIAL] = w.reshape(4, 2, P, 384).transpose(0, 2, 1, 3).reshape(4, P, PARTIAL)
    return u


def _gated_units(w1, w3, w2, steps_first):
    ups = [_up_units(w) for w in ((w1, w3) if w3 is not None else (w1,))]
    dn = _down_units(w2)
    n = dn.shape[0]
    out = [u[0] for u in ups]
    for s in range(n):
        if s + 1 < n:
            out += [u[s + 1] for u in ups]
        out.append(dn[s])
    return np.stack(out)


def _chunks(v):
    return v.reshape(-1, P).T


def _layout(i):
    w_in, units = i["ev_w_in"][0], []
    mixed = [_up_units(w_in[:, 1536:2048]), _up_units(w_in[:, 2048:2560]), _down_units(w_in[:, 0:1024]),
             _down_units(w_in[:, 1024:1536], 512), _down_units(i["ev_w_out"][0])]
    units += mixed
    for l in range(2):
        if l == 1:
            units.append(i["od_pool_w"][0].reshape(4, 2, P, 256).transpose(2, 0, 1, 3).reshape(1, P, UNIT))
        kv = i["xa_w_kv"][l]
        units += [_down_units(kv[:, 0:1024]), _down_units(i["xa_w_q"][l]), _down_units(kv[:, 1024:2048]),
                  _down_units(i["xa_w_o"][l]), _gated_units(i["mlp_w1"][l], None, i["mlp_w2"][l], True)]
    order = [0, 3, 1, 4, 2, 5]
    for l in range(2):
        w = i["w_in_2"][l]
        q = w[:, 768:1152].reshape(D, 6, 64)[:, order].reshape(D, 384)
        qk = np.concatenate([q, w[:, 1152:1280]], 1)
        mv = np.concatenate([w[:, 1408:1664], w[:, 1280:1408]], 1)
        wo = i["w_out_2"][l]
        wo = np.concatenate([wo[0:384], wo[384:768].reshape(6, 64, D)[order].reshape(384, D), wo[768:]], 0)
        units += [_gated_units(i["ffn1_w1_2"][l], i["ffn1_w3_2"][l], i["ffn1_w2_2"][l], True),
                  _up_units(w[:, 0:768]), _down_units(qk, 512), _narrow_units(mv),
                  _down_units(i["w_mem_kv_2"][l], 512), _down_units(wo),
                  _gated_units(i["ffn2_w1_2"][l], i["ffn2_w3_2"][l], i["ffn2_w2_2"][l], True)]
    units.append(np.zeros((AHEAD, P, UNIT), np.float32))
    weights = np.concatenate(units, 0)

    small = np.zeros((P, N_SMALL), np.float32)
    def put(dst, table, name, v):
        dst[:, table[name]] = v
    put(small, SMALL, "mem_g", _chunks(i["mem_norm_g"]))
    for l in range(2):
        put(small, SMALL, f"mix_g{l}", _chunks(i["mix_norm_g"][l]))
        put(small, SMALL, f"xat_g{l}", _chunks(i["xattn_norm_g"][l]))
        put(small, SMALL, f"mlp_g{l}", _chunks(i["mlp_norm_g"][l]))
        put(small, SMALL, f"xq{l}", np.tile(_chunks(i["xa_q_norm_g"][l]), (1, 2)))
        put(small, SMALL, f"xk{l}", np.tile(_chunks(i["xa_k_norm_g"][l]), (1, 2)))
    put(small, SMALL, "ev_q", np.tile(_chunks(i["ev_q_norm_g"][0]), (1, 4)))
    put(small, SMALL, "ev_k", np.tile(_chunks(i["ev_k_norm_g"][0]), (1, 4)))
    put(small, SMALL, "conv_w", i["ev_conv_w"][0].reshape(4, 4, P).transpose(2, 0, 1).reshape(P, 16))
    put(small, SMALL, "conv_b", _chunks(i["ev_conv_b"][0]))
    put(small, SMALL, "ga_b", _chunks(i["ev_gate_a_b"][0]))
    put(small, SMALL, "gx_b", _chunks(i["ev_gate_x_b"][0]))
    put(small, SMALL, "lam", _chunks(i["ev_lambda"][0]))
    gates = np.concatenate([i["ev_gate_a_w"][0], i["ev_gate_x_w"][0]], 0).transpose(1, 0, 2).reshape(P, 1024)

    layers = np.zeros((2, P, N_LAYER), np.float32)
    for l in range(2):
        d = layers[l]
        put(d, LAYER, "ffn1_g", _chunks(i["ffn1_norm_2"][l]))
        put(d, LAYER, "mix_g", _chunks(i["mix_norm_2"][l]))
        put(d, LAYER, "mem_g", _chunks(i["mem_norm_2"][l]))
        put(d, LAYER, "ffn2_g", _chunks(i["ffn2_norm_2"][l]))
        put(d, LAYER, "conv_w", i["conv_w_2"][l].reshape(31, 3, P).transpose(2, 0, 1).reshape(P, 93))
        put(d, LAYER, "conv_b", _chunks(i["conv_b_2"][l]))
        put(d, LAYER, "ln_g", _chunks(i["conv_ln_g_2"][l]))
        put(d, LAYER, "ln_b", _chunks(i["conv_ln_b_2"][l]))
        put(d, LAYER, "sinks", i["swa_sinks_2"][l][order])
        put(d, LAYER, "mq_g", np.tile(i["mem_q_norm_2"][l], 2)[:, None])
        put(d, LAYER, "mk_g", np.tile(i["mem_k_norm_2"][l], 2)[:, None])
        put(d, LAYER, "qk_g", np.concatenate([np.tile(i["swa_q_norm_2"][l], 6), np.tile(i["swa_k_norm_2"][l], 2)]))
        put(d, LAYER, "final_g", i["final_norm_2"][l])

    qi, kj = np.arange(S)[:, None], np.arange(S)[None, :]
    def masked(m):
        return np.where(m, 0.0, BIG).astype(np.float32).reshape(NT, P, S).transpose(1, 0, 2).reshape(P, 512)
    near = (qi >= kj) & (qi - kj <= 128)
    by4, by16 = ((qi >= kj) & ((qi - kj) % r == 0) for r in (4, 16))
    cnt = (near.astype(np.float32) + by4 + by16).astype(np.float32)
    const = np.zeros((P, N_CONST), np.float32)
    put(const, CONST, "ident", np.eye(P))
    put(const, CONST, "ones", 1.0)
    put(const, CONST, "neg1", masked(cnt > 0))
    put(const, CONST, "cnt", cnt.reshape(NT, P, S).transpose(1, 0, 2).reshape(P, 512))
    put(const, CONST, "neg2", masked((qi >= kj) & (qi - kj < 128)))
    freq = np.float32(10000.0) ** (-np.arange(0, 64, 2, dtype=np.float32) / np.float32(64))
    put(const, CONST, "freq", freq)
    tt, ss = np.arange(S)[None, :], np.arange(S)[:, None]
    pool = np.zeros((S, 4, S), np.float32)
    for g, w in enumerate((2, 4, 8, 16)):
        inside = (ss <= tt) & (ss > tt - w)
        pool[:, g, :] = inside / np.minimum(tt + 1, w) - (ss == tt)
    pool = pool.reshape(NT, P, 4, S).transpose(1, 0, 2, 3).reshape(P, 2048)
    return {
        "weights": weights, "small": small, "const": const, "layer_par": layers, "gates": np.ascontiguousarray(gates),
        "pool_mat": pool, "scale_row": np.ascontiguousarray(np.broadcast_to(i["od_scale"][0], (P, D))),
        "x_in": i["x"][0], "mem1": i["mem"][0], "mem2": i["mem_2"][0],
        "pos": np.ascontiguousarray(i["positions_2"][0].reshape(NT, P).T),
    }


def kernel(**inputs):
    import concourse.bacc as bacc
    from concourse.bass_utils import run_bass_kernel_spmd

    arrays = _layout({k: np.asarray(v) for k, v in inputs.items()})
    steps = {}
    for attempt in range(2):
        nc = bacc.Bacc("TRN2", target_bir_lowering=False, num_devices=1)
        args = {n: nc.dram_tensor(f"{n}_dram", a.shape, mybir.dt.from_np(a.dtype), kind="ExternalInput").ap()
                for n, a in arrays.items()}
        out = nc.dram_tensor("out_dram", (S, D), F32, kind="ExternalOutput").ap()
        build_program(nc, steps, out=out, **args)
    r = run_bass_kernel_spmd(nc, [{f"{n}_dram": a for n, a in arrays.items()}], core_ids=[0])
    return r.results[0]["out_dram"].reshape(1, S, D)
```

```python
from contextlib import ExitStack

import concourse.bass as bass
from concourse import mybir
import numpy as np

F32, F32R, I32 = mybir.dt.float32, mybir.dt.float32r, mybir.dt.int32
ACT, ALU, AX = mybir.ActivationFunctionType, mybir.AluOpType, mybir.AxisListType

P = 128
S, D = 256, 1024
NT, KC = S // P, D // P
EPS = 1e-6
UNIT = 2048
SLOTS = 3
AHEAD = SLOTS - 1
D_FF, D_FF2 = 4096, 2816
FF = 256
PARTIAL = 768
BIG = -1e30

def _columns(widths):
    at, out = 0, {}
    for name, w in widths:
        out[name] = slice(at, at + w)
        at += w
    return out, at

SMALL, N_SMALL = _columns([
    ("mix_g1", KC),
    ("ev_q", 4), ("ev_k", 4), ("conv_w", 16), ("conv_b", 4), ("ga_b", 4), ("gx_b", 4), ("lam", 4),
    ("xq0", 4), ("xq1", 4), ("xk0", 4), ("xk1", 4)])
LAYER, N_LAYER = _columns([
    ("conv_w", 93), ("conv_b", 3), ("ln_g", 3),
    ("ln_b", 3), ("sinks", 6), ("mq_g", 2), ("mk_g", 2), ("qk_g", 512)])
GAINS1 = ["mix0", "mem", "xat0", "mlp0", "xat1", "mlp1"]
GAINS2 = ["ffn1", "mem", "mix", "ffn2", "final"]
ROW1 = {name: i for i, name in enumerate(GAINS1)}
ROW2 = {name: i for i, name in enumerate(GAINS2)}
FIRST2 = len(GAINS1)
CONST, N_CONST = _columns([("ident", P), ("ones", P), ("neg1", 512), ("cnt", 512), ("neg2", 512), ("freq", 32)])


class Count:

    def __init__(self, base=0, steps=None):
        self.base, self.steps = base, dict(steps or {})

    def plus(self, n):
        return Count(self.base + n, self.steps)

    def same_steps(self, other):
        return self.steps == other.steps


class Lane:

    def __init__(self, prog, name, eng):
        self.prog, self.name, self.eng, self.seen = prog, name, eng, {}

    def after(self, *tokens):
        need = {}
        for sem, value in tokens:
            best = need.get(sem)
            if best is None or (best.same_steps(value) and value.base > best.base):
                need[sem] = value
            elif not best.same_steps(value):
                self._wait(sem, value)
        for sem, value in need.items():
            self._wait(sem, value)
        return self.eng

    def _wait(self, sem, value):
        known = self.seen.get(sem)
        if known is not None and known.same_steps(value) and known.base >= value.base:
            return
        if not value.steps and value.base <= 0:
            return
        self.seen[sem] = value
        self.eng.wait_ge(self.prog.sems[sem], self.prog.value(value, self.eng))

    def did(self, inst, sem=None, n=1):
        sem = sem or self.name
        inst.then_inc(self.prog.sems[sem], n)
        self.prog.counts[sem] = self.prog.counts[sem].plus(n)
        return (sem, self.prog.counts[sem])


class Program:

    def __init__(self, nc, sems, steps):
        self.nc, self.sems, self.steps = nc, sems, steps
        self.counts = {s: Count() for s in sems}
        self.counts["unit"] = Count()
        self.live, self.vars, self.n_loops = {}, {}, 0
        self.lanes = []

    def value(self, count, eng=None):
        v = count.base
        for var, step in count.steps.items():
            v = self.vars[var] * step + v
        return v

    def loop(self, n, body):
        me = self.n_loops
        self.n_loops += 1
        steps, tails = self.steps.get(me, ({}, {}))
        entry, before = dict(self.counts), dict(self.live)
        for s in self.counts:
            if steps.get(s):
                self.counts[s] = Count(entry[s].base, {**entry[s].steps, me: steps[s]})
        start = dict(self.counts)
        for key, tail in tails.items():
            rel, out = {}, []
            for sem, value in before.get(key, []):
                if value.same_steps(entry[sem]):
                    rel[sem] = max(rel.get(sem, -10**9), value.base - entry[sem].base)
                else:
                    out.append((sem, value))
            for sem, r in tail:
                rel[sem] = max(rel.get(sem, -10**9), r - steps.get(sem, 0))
            self.live[key] = out + [(sem, start[sem].plus(r)) for sem, r in rel.items()]
        started = dict(self.live)
        with self.nc.Fori(0, n) as it:
            self.vars[me] = it
            body()
        for lane in self.lanes:
            lane.seen = {}
        found = {s: self.counts[s].base - entry[s].base for s in self.counts}
        tails = {key: [(sem, v.base - entry[sem].base) for sem, v in toks if v.same_steps(start[sem])]
                 for key, toks in self.live.items() if toks is not started.get(key)}
        self.steps[me] = (found, tails)
        for s in self.counts:
            self.counts[s] = Count(entry[s].base + n * found[s], entry[s].steps)
        for key in tails:
            self.live[key] = [(sem, Count(v.base + (n - 1) * found[sem], entry[sem].steps)
                               if v.same_steps(start[sem]) else v) for sem, v in self.live[key]]


def build_program(nc, steps, weights, small, const, layer_par, gains, gates, pool_mat, scale_row, x_in, mem1, mem2,
                  pos, out):
    with ExitStack() as ctx:
        def sb(name, shape, dt=F32):
            return ctx.enter_context(nc.sbuf_tensor(name, shape, dt))

        names = ["act", "dve", "pe", "pool", "d_x0", "d_x1", "d_mem", "d_small", "d_ident", "d_const", "d_gates", "d_pos", "d_par",
                 "d_pool", "d_mem2", "d_gain", "d_mgain", "d_out"] + [f"d_w{i}" for i in range(SLOTS)]
        prog = Program(nc, {n: ctx.enter_context(nc.semaphore(n)) for n in names}, steps)
        A, V, T, G, SP = (Lane(prog, n, e) for n, e in (("act", nc.scalar), ("dve", nc.vector), ("pe", nc.tensor),
                                                        ("pool", nc.gpsimd), ("sp", nc.sync)))
        prog.lanes = [A, V, T, G, SP]
        live = prog.live

        raw = sb("raw", [P, SLOTS, UNIT])
        w_hi = sb("w_hi", [P, SLOTS, UNIT], F32R)
        w_lo = sb("w_lo", [P, SLOTS, UNIT], F32R)
        x = sb("x", [P, NT, D])
        xT = sb("xT", [P, KC, 2, S], F32R)
        memT = sb("memT", [P, KC, 2, S], F32R)
        hT = sb("hT", [P, 3, 2, 2, S], F32R)
        arena = sb("arena", [P, 16, 1024])
        par = sb("par", [P, max(N_LAYER, 1024)])
        sm = sb("sm", [P, N_SMALL])
        cst = sb("cst", [P, N_CONST])
        gain_row = sb("gain_row", [P, D])
        stat = sb("stat", [P, 96])
        mhalf = sb("mhalf", [P, 12])
        rg = sb("rg", [P, 8, 4])
        trig = sb("trig", [P, 2, NT, 32])
        ps = ctx.enter_context(nc.psum_tensor("ps", [P, 8, 512], F32))

        def c(name):
            return cst[:, CONST[name]]

        def slot2(a):
            return arena[:, a:a + 2, :]

        ident = c("ident")

        def last_of(key):
            return live.get(key, [])

        class Stream:
            seq, taken, plan, pitch = 0, 0, [], 0

        st = Stream()
        WHOLE, ON_POOL, NARROW = (UNIT, V, nc.vector), (UNIT, G, nc.gpsimd), (PARTIAL, V, nc.vector)

        def prefetch():
            s = st.seq % SLOTS
            st.seq += 1
            width, lane, eng = st.plan.pop(0) if st.plan else WHOLE
            nr = prog.value(prog.counts["unit"])
            prog.counts["unit"] = prog.counts["unit"].plus(1)
            src = weights[bass.ds(nc.sync.snap(nr), 1), :, 0:width].rearrange("a p n -> (a p) n") \
                if prog.counts["unit"].steps else weights[nr, :, 0:width]
            SP.after(*last_of(("raw", s)))
            loaded = SP.did(nc.sync.dma_start(raw[:, s, 0:width], src), f"d_w{s}", 16)
            A.after(loaded, *last_of(("slot", s)))
            hi = A.did(nc.scalar.activation(w_hi[:, s, 0:width], raw[:, s, 0:width], ACT.Copy))
            lane.after(hi)
            lo = lane.did(eng.tensor_tensor(w_lo[:, s, 0:width], raw[:, s, 0:width],
                                            w_hi[:, s, 0:width].bitcast(F32), ALU.subtract))
            live["raw", s] = [lo]
            live["unit", s] = [lo]

        def take():
            s = st.taken % SLOTS
            st.taken += 1
            T.after(*live["unit", s])
            return s

        def release(s, last, refill=True):
            tok = T.did(last)
            live["slot", s] = [tok]
            if refill:
                prefetch()
            background_step()
            return tok

        def plan(kinds):
            assert not st.plan and all(kind == WHOLE for kind in kinds[:AHEAD])
            st.plan = list(kinds[AHEAD:])

        def need(ready, t, k):
            if ready is not None:
                T.after(ready[t, k // 4])

        def cols_tile(bank, s, src, half, ready, ts=None):
            T.after(*last_of(("bank", bank)))
            wv = [w[:, s, :].rearrange("p (k n) -> p k n", k=KC) for w in (w_hi, w_lo)]
            cs = slice(half * P, half * P + P)
            tiles = range(NT) if ts is None else [ts]
            tok = slice(0, S) if ts is None else slice(ts * P, ts * P + P)
            out2 = ps[:, bank, :].rearrange("p (a t) -> p a t", a=2)
            for k in range(KC):
                for t in tiles:
                    need(ready, t, k)

                def hi():
                    return nc.tensor.matmul(out2[:, :, tok], wv[0][:, k, cs], src[:, k, :, tok], start=(k == 0),
                                            stop=(k == KC - 1))

                def lo():
                    if ts is None:
                        return nc.tensor.matmul(out2[:, 0, :], wv[1][:, k, cs], src[:, k, 0, :], start=False, stop=False)
                    return nc.tensor.matmul(out2[:, :, tok], wv[1][:, k, cs], src[:, k, :, tok], start=False,
                                            stop=False)
                if k == 0:
                    hi()
                    last = lo()
                else:
                    lo()
                    last = hi()
            return last

        def rows_tile(bank, t, s, at, n, lhs, first, last_k):
            for j, (h, l, ready) in enumerate(lhs):
                cs = slice(at + j * st.pitch, at + j * st.pitch + n)
                ts = slice(t * P, t * P + P)
                if ready is not None:
                    T.after(ready[t])
                nc.tensor.matmul(ps[:, bank, 0:n], h[:, ts], w_hi[:, s, cs], start=(first and j == 0), stop=False)
                nc.tensor.matmul(ps[:, bank, 0:n], h[:, ts], w_lo[:, s, cs], start=False, stop=False)
                last = nc.tensor.matmul(ps[:, bank, 0:n], l[:, ts], w_hi[:, s, cs], start=False,
                                        stop=(last_k and j == len(lhs) - 1))
            return last

        def chunk(src, k, ready):
            if ready is None:
                return src[:, k, 0, :], src[:, k, 1, :], None
            toks = {t: ready["chunk", k] if ("chunk", k) in ready else ready[t, k // 4] for t in range(NT)}
            return src[:, k, 0, :], src[:, k, 1, :], toks

        def rows_unit(base, lhs, halves, n, first, last_k):
            s = take()
            st.pitch = halves * n
            ends = []
            for t in range(NT):
                for h in range(halves):
                    bank = base + halves * t + h
                    if first:
                        T.after(*last_of(("bank", bank)))
                    last = rows_tile(bank, t, s, h * n, n, lhs, first, last_k)
                if t == 0:
                    ends.append(T.did(last))
            ends.append(release(s, last))
            return ends

        def project(base, src, halves, n, per_unit, ready, part=(0, KC)):
            for k in range(*part, per_unit):
                ends = rows_unit(base, [chunk(src, k + j, ready) for j in range(per_unit)], halves, n,
                                 k == 0, k + per_unit == KC)
            return ends

        def project_late_tile(base, src, ready, order, late=None):
            n = 512

            def pair(i):
                return [chunk(src, k, ready) for k in order[2 * i:2 * i + 2]]
            for i in range(2):
                rows_unit(base, pair(i), 2, n, i == 0, False)
            finish_background()
            ready.update(late or {})
            prefetch()
            slots, ends = [take(), take()], []
            st.pitch = 2 * n
            for t in range(NT):
                for i, s in enumerate(slots):
                    for h in range(2):
                        last = rows_tile(base + 2 * t + h, t, s, h * n, n, pair(2 + i), False, i == 1)
                    if t == 1:
                        tok = release(s, last, refill=(i == 0))
                if t == 0:
                    ends.append(T.did(last))
                    normed_0 = normed_tile(0, 1.0, (base, ends), slot2(6))
            live["xT"] = live["mix_end"] = [tok]
            return base, [*ends, tok], normed_0

        background = []

        def in_background(steps):
            background.append(steps)

        def background_step():
            for steps in list(background):
                if next(steps, "end") == "end":
                    background.remove(steps)

        def finish_background():
            while background:
                background_step()

        def recip_root(dst, src, n, scale, after):
            V.after(*after)
            ms = V.did(nc.vector.tensor_scalar(dst, src, scale, EPS, ALU.mult, ALU.add))
            G.after(ms, half_ready)
            return G.did(nc.gpsimd.tensor_tensor(dst, dst, mhalf[:, 0:n], ALU.pow))

        def transpose_rows(rows, t, n_chunks, bank0, wait):
            toks = []
            for b in range(0, n_chunks, 4):
                bank = bank0 + b // 4
                T.after(*wait, *last_of(("bank", bank)), ident_ready)
                for j in range(min(4, n_chunks - b)):
                    last = nc.tensor.transpose(ps[:, bank, j * P:j * P + P], rows[:, (b + j) * P:(b + j + 1) * P], ident)
                toks.append(T.did(last))
            return toks

        def split(dst_hi, dst_lo, src, wait):
            A.after(*wait)
            hi = A.did(nc.scalar.activation(dst_hi, src, ACT.Copy))
            V.after(hi, *wait)
            return V.did(nc.vector.tensor_tensor(dst_lo, src, dst_hi.bitcast(F32), ALU.subtract))

        def gain_source(row):
            if isinstance(row, int):
                return gains[row:row + 1, :].broadcast_to([P, D])
            return gains[bass.ds(nc.scalar.snap(row), 1), :].broadcast_to([P, D])

        def load_gain(row):
            src = gain_source(row)
            A.after(*last_of("gain_read"))
            live["gain"] = [A.did(nc.scalar.dma_start(gain_row[:, :], src), "d_gain", 16)]

        def norm_begin(t, src, junk, st0, wait):
            ss = stat[:, st0 + t:st0 + t + 1]
            A.after(*wait, *last_of("junk"), *last_of(("stat", st0 + t)))
            sq = A.did(nc.scalar.activation(junk, src[:, t, :], ACT.Square, accum_out=ss))
            live["junk"] = [sq]
            return recip_root(ss, ss, 1, 1.0 / D, [sq])

        def norm_end(t, dst, src, st0, root, gain, wait):
            ss, toks = stat[:, st0 + t:st0 + t + 1], []
            for b in range(2):
                hs = slice(512 * b, 512 * b + 512)
                V.after(root, *wait)
                if gain is None:
                    toks.append(V.did(nc.vector.tensor_scalar(dst[:, t, hs], src[:, t, hs], ss, None, ALU.mult)))
                else:
                    toks.append(V.did(nc.vector.scalar_tensor_tensor(dst[:, t, hs], src[:, t, hs], ss, gain[:, hs],
                                                                     ALU.mult, ALU.mult)))
            live["stat", st0 + t] = [toks[1]]
            return toks

        def tile_to_cols(dst, rows, t, bank0, wait, key):
            ready = {}
            for b in range(2):
                bank = bank0 + 2 * t + b
                T.after(wait[b], *last_of(("bank", bank)), ident_ready)
                for j in range(4):
                    cs = slice(512 * b + j * P, 512 * b + (j + 1) * P)
                    last = nc.tensor.transpose(ps[:, bank, j * P:j * P + P], rows[:, t, cs], ident)
                tr = T.did(last)
                pv = ps[:, bank, :].rearrange("p (k n) -> p k n", k=4)
                ks, ts = slice(4 * b, 4 * b + 4), slice(t * P, t * P + P)
                ready[t, b] = split(dst[:, ks, 0, ts], dst[:, ks, 1, ts], pv, [tr, *last_of(key)])
                live["bank", bank] = [ready[t, b]]
            return ready

        def evac_cols(dst, ks, ts, bank, n, gain, tmp, wait, key):
            m = 512 // n
            pv = ps[:, bank, :].rearrange("p (k n) -> p k n", k=m)
            tv = tmp.rearrange("p (k n) -> p k n", k=m)
            V.after(*wait, *last_of(key))
            g = V.did(nc.vector.tensor_tensor(tv, pv, gain.unsqueeze(2).broadcast_to([P, m, n]), ALU.mult))
            live["bank", bank] = [g]
            return split(dst[:, ks, 0, ts], dst[:, ks, 1, ts], tv, [g, *last_of(key)])

        def head_norms(jobs, heads, width, st0, wait, gain_row=None):
            def hv(ap):
                return ap.rearrange("p (h c) -> p h c", h=heads)
            squares, roots, toks = [], [], []
            before = last_of("junk")
            for dst, src, junk, ready, banks in jobs:
                A.after(ready, *wait, *before)
                squares.append(A.did(nc.scalar.activation(junk, src, ACT.Square)))
            for i, (dst, src, junk, ready, banks) in enumerate(jobs):
                ss = stat[:, st0 + i * heads:st0 + (i + 1) * heads]
                V.after(squares[i], *wait)
                su = V.did(nc.vector.tensor_reduce(ss, hv(junk), AX.X, ALU.add))
                roots.append(recip_root(ss, ss, heads, 1.0 / width, [su]))
            for i, (dst, src, junk, ready, banks) in enumerate(jobs):
                ss = stat[:, st0 + i * heads:st0 + (i + 1) * heads]
                V.after(roots[i])
                tok = V.did(nc.vector.tensor_tensor(hv(dst), hv(src), ss.unsqueeze(2).broadcast_to([P, heads, width]),
                                                    ALU.mult))
                for bank in banks:
                    live["bank", bank] = [tok]
                toks.append(tok)
            live["junk"] = [toks[-1]]
            if gain_row is not None:
                for i, job in enumerate(jobs):
                    V.after(toks[i])
                    toks[i] = V.did(nc.vector.tensor_tensor(job[0], job[0], gain_row, ALU.mult))
            return toks

        def rows_to_cols(dst, rows, n_chunks, gain, banks, wait):
            out_toks = []
            for t in range(NT):
                toks = transpose_rows(rows[t], t, n_chunks, banks(t), [wait[t]])
                for b, tok in enumerate(toks):
                    m = min(4, n_chunks - 4 * b)
                    pv = ps[:, banks(t) + b, 0:m * P].rearrange("p (k n) -> p k n", k=m)
                    dv = dst[:, 4 * b:4 * b + m, t * P:t * P + P]
                    if gain is None:
                        A.after(tok, *wait)
                        g = A.did(nc.scalar.activation(dv, pv, ACT.Copy))
                    else:
                        V.after(tok)
                        g = V.did(nc.vector.tensor_tensor(dv, pv, gain[:, 4 * b:4 * b + m].unsqueeze(2)
                                                          .broadcast_to([P, m, P]), ALU.mult))
                    live["bank", banks(t) + b] = [g]
                    out_toks.append(g)
            return out_toks

        def attention(heads, p_buf, pt_buf, wait, st0, key, base, n_banks=4):
            scored, pend, outs = {}, [], {}
            other = 4 - base
            halves = [slice(0, S), slice(S, 2 * S)]

            def scores(i):
                hd, bank = heads[i], base + i % n_banks
                T.after(*wait, *hd.get("wait", ()), *last_of(("bank", bank)))
                masked = hd.get("neg") is not None
                if masked:
                    T.after(mask_ready)
                    nc.tensor.matmul(ps[:, bank, :], ident_b[:, :], hd["neg"], start=True, stop=False)
                for t in range(NT):
                    for j, (q, k) in enumerate(zip(hd["q"], hd["k"])):
                        last = nc.tensor.matmul(ps[:, bank, halves[t]], q[:, t * P:t * P + P], k,
                                                start=(j == 0 and not masked),
                                                stop=(j == len(hd["q"]) - 1 and (t == 1 or not masked)))
                scored[i] = T.did(last)

            def exponentials(i):
                hd, bank, b = heads[i], base + i % n_banks, i % 2
                src = ps[:, bank, :].rearrange("p (t n) -> p t n", t=NT)
                pb = p_buf[:, b * 512:b * 512 + 512].rearrange("p (t n) -> p t n", t=NT)
                at = st0 + 8 * b
                nm, den, sk = stat[:, at:at + 2], stat[:, at + 2:at + 4], stat[:, at + 4:at + 6]
                V.after(scored[i], *last_of((key, "st", b)))
                sink = hd.get("sink")
                m = V.did(nc.vector.tensor_reduce(nm, src, AX.X, ALU.max, negate=sink is None))
                if sink is not None:
                    V.after(m)
                    m = V.did(nc.vector.tensor_scalar(nm, nm, sink, -1.0, ALU.max, ALU.mult))
                A.after(m, *last_of((key, "p", b)))
                for t in range(NT):
                    e = A.did(nc.scalar.activation(pb[:, t, :], src[:, t, :], ACT.Exp, bias=nm[:, t:t + 1],
                                                   accum_out=den[:, t:t + 1]))
                live["bank", bank] = [e]
                if sink is not None:
                    e = A.did(nc.scalar.activation(sk, nm, ACT.Exp, bias=sink))
                return pb, den, sk, e

            def normalized(i, pb, den, sk, e):
                hd, b = heads[i], i % 2
                sink = hd.get("sink")
                V.after(e)
                if hd.get("cnt") is not None:
                    for t in range(NT):
                        e = V.did(nc.vector.scalar_tensor_tensor(pb[:, t, :], pb[:, t, :], 1.0, hd["cnt"][:, halves[t]],
                                                                 ALU.mult, ALU.mult, accum_out=den[:, t:t + 1]))
                    V.after(e)
                if sink is not None:
                    e = V.did(nc.vector.tensor_tensor(den, den, sk, ALU.add))
                    V.after(e)
                r = V.did(nc.vector.reciprocal(den, den))
                V.after(r)
                for t in range(NT):
                    pn = V.did(nc.vector.tensor_scalar(pb[:, t, :], pb[:, t, :], den[:, t:t + 1], None, ALU.mult))
                live[key, "st", b] = [pn]
                return pb, pn

            def value(i, pb, pn):
                hd, b = heads[i], i % 2
                bank = other + b
                T.after(pn, ident_ready, *last_of(("bank", bank)))
                for t in range(NT):
                    for mm in range(NT):
                        last = nc.tensor.transpose(ps[:, bank, mm * S + t * P:mm * S + t * P + P],
                                                   pb[:, t, mm * P:mm * P + P], ident)
                tr = T.did(last)
                live[key, "p", b] = [tr]
                ptb = pt_buf[:, b * 512:b * 512 + 512]
                A.after(tr, *last_of((key, "pt", b)))
                cp = A.did(nc.scalar.activation(ptb, ps[:, bank, :], ACT.Copy))
                live["bank", bank] = [cp]
                pend.append((i, ptb, cp))

            def product():
                i, ptb, cp = pend.pop(0)
                hd, b = heads[i], i % 2
                bank = other + 2 + hd["bank"]
                T.after(cp, *hd.get("v_wait", ()))
                if hd["open"]:
                    T.after(*last_of(("bank", bank)))
                for cc, (p0, p1, off) in enumerate(hd["place"]):
                    for mm in range(NT):
                        last = nc.tensor.matmul(ps[p0:p1, bank, off:off + S], hd["v"](mm, cc),
                                                ptb[:, mm * S:mm * S + S], start=(mm == 0), stop=(mm == NT - 1))
                pv = T.did(last)
                live[key, "pt", b] = [pv]
                if hd["close"] is not None:
                    ks, n = hd["close"]
                    src = ps[:, bank, 0:n * S].rearrange("p (k n) -> p k n", k=n)
                    tok = split(xT[:, ks, 0, :], xT[:, ks, 1, :], src, [pv, *last_of("xT")])
                    live["bank", bank] = [tok]
                    for k in range(ks.start, ks.stop):
                        outs["chunk", k] = tok

            n = len(heads)
            for i in range(min(n_banks, n)):
                scores(i)
            following = exponentials(0)
            for i in range(n):
                begun = following
                if i + 1 < n:
                    following = exponentials(i + 1)
                pb, pn = normalized(i, *begun)
                background_step()
                if i >= 1:
                    product()
                value(i, pb, pn)
                if i + n_banks < n:
                    scores(i + n_banks)
            product()
            return outs

        def add_rows(t, factor, product):
            base, ends = product[0:2]
            toks = []
            for h in range(2):
                bank, xs = base + 2 * t + h, x[:, t, h * 512:h * 512 + 512]
                V.after(ends[t], *last_of(("x", t)))
                if factor == 1.0:
                    tok = V.did(nc.vector.tensor_tensor(xs, ps[:, bank, :], xs, ALU.add))
                else:
                    tok = V.did(nc.vector.scalar_tensor_tensor(xs, ps[:, bank, :], factor, xs, ALU.mult, ALU.add))
                live["bank", bank] = [tok]
                toks.append(tok)
            live["x", t] = toks

        def all_x():
            return [*live["x", 0], *live["x", 1]]

        def sum_halves(dst, tmp, bank, wait, key):
            pv = ps[:, bank:bank + 2, :]
            A.after(*wait, *last_of(key))
            b = A.did(nc.scalar.activation(tmp, pv[:, :, S:2 * S], ACT.Copy))
            V.after(b, *wait, *last_of(key))
            tok = V.did(nc.vector.tensor_tensor(dst, pv[:, :, 0:S], tmp, ALU.add))
            live["bank", bank] = [tok]
            live["bank", bank + 1] = [tok]
            return tok

        def buf(a, j=0):
            return arena[:, a, 512 * j:512 * j + 512].rearrange("p (k n) -> p k n", k=2)

        def up_unit(bank, ready, tiles=None):
            s = take()
            if tiles is None:
                for h in range(2):
                    last = cols_tile(bank + h, s, xT, h, ready)
            else:
                for t in range(NT):
                    if t:
                        tiles()
                    for h in range(2):
                        last = cols_tile(bank + h, s, xT, h, ready, t)
            return release(s, last)

        def up_relu2(hb, ready, tiles=None):
            tok = up_unit(0, ready, tiles)
            z = sum_halves(buf(1, 0), buf(0, 0), 0, [tok], "ff_z")
            V.after(z, *last_of("ff_h"))
            h = V.did(nc.vector.scalar_tensor_tensor(buf(2, 0), buf(1, 0), 0.0, buf(1, 0), ALU.max, ALU.mult))
            live["ff_z"] = [h]
            tok = split(hT[:, hb, :, 0, :], hT[:, hb, :, 1, :], buf(2, 0), [h, *last_of(("hT", hb))])
            live["ff_h"] = [tok]
            live["h", hb] = [tok]

        def up_swiglu(hb, ready, tiles=None):
            tok = up_unit(0, ready, tiles)
            g = sum_halves(buf(1, 0), buf(0, 0), 0, [tok], "ff_z")
            A.after(g, *last_of("ff_g"))
            sg = A.did(nc.scalar.activation(buf(2, 0), buf(1, 0), ACT.Sigmoid))
            V.after(sg, *last_of("ff_g"))
            gs = V.did(nc.vector.tensor_tensor(buf(3, 0), buf(1, 0), buf(2, 0), ALU.mult))
            live["ff_z"] = [gs]
            tok = up_unit(2, ready)
            u = sum_halves(buf(4, 0), buf(0, 1), 2, [tok], "ff_u")
            V.after(u, gs, *last_of("ff_h"))
            h = V.did(nc.vector.tensor_tensor(buf(5, 0), buf(3, 0), buf(4, 0), ALU.mult))
            live["ff_g"] = [h]
            live["ff_u"] = [h]
            tok = split(hT[:, hb, :, 0, :], hT[:, hb, :, 1, :], buf(5, 0), [h, *last_of(("hT", hb))])
            live["ff_h"] = [tok]
            live["h", hb] = [tok]

        def down(hb, last_k):
            ready = dict.fromkeys(range(NT), live["h", hb][0])
            ends = rows_unit(4, [(hT[:, hb, j, 0, :], hT[:, hb, j, 1, :], ready) for j in range(2)], 2, 512, False, last_k)
            live["hT", hb] = [ends[1]]
            return ends

        def x_begin(t, factor, product):
            if product is not None:
                add_rows(t, factor, product)
            return norm_begin(t, x, arena[:, 8, :], 0, last_of(("x", t)))

        def x_end(t, root, dst, gain=True):
            toks = norm_end(t, dst, x, 0, root, gain_row if gain else None,
                            [*last_of(("x", t)), *(last_of("gain") if gain else [])])
            if t == 1 and gain:
                live["gain_read"] = [toks[1]]
            return toks

        def normed_tile(t, factor, product, dst):
            return x_end(t, x_begin(t, factor, product), dst)

        def normed_pair(factor, product, dst, gain=True):
            for t in range(NT):
                if product is not None:
                    add_rows(t, factor, product)
            roots = [x_begin(t, factor, None) for t in range(NT)]
            return [x_end(t, roots[t], dst, gain) for t in range(NT)]

        def feed_forward(factor_in, product, wide, up, per_body, next_gain, bank=0, tile_done=None, beside=None,
                         before_last=None):
            rows, ready = slot2(6), {}
            normed = normed_pair(1.0, None, rows) if product is None else {}

            def one(t):
                if product is not None:
                    normed[t] = normed_tile(t, factor_in, product, rows) if t else product[2]
                ready.update(tile_to_cols(xT, rows, t, bank, normed[t], "xT"))
            one(0)

            def second():
                one(1)
                if tile_done:
                    tile_done()
                for b in range(4):
                    T.after(*last_of(("bank", 4 + b)), zero_ready)
                    nc.tensor.matmul(ps[:, 4 + b, :], zero[:, 0:P], zero[:, :], start=True, stop=False)
            up(0, ready, second)
            load_gain(next_gain)
            if beside:
                beside()
            n = wide // FF - 1
            assert n % per_body == 0

            def body():
                for j in range(per_body):
                    up((j + 1) % per_body, None)
                    down(j, False)
            prog.loop(n // per_body, body)
            if before_last:
                before_last()
            ends = down(0, True)
            live["xT"] = [ends[1]]
            return 4, ends

        zero = sb("zero", [P, 512], mybir.dt.bfloat16)
        half_ready = G.did(nc.gpsimd.memset(mhalf[:, :], -0.5))
        zero_ready = G.did(nc.gpsimd.memset(zero[:, :], 0.0))

        ident_b = sb("ident_b", [P, P], mybir.dt.bfloat16)
        neg_b = sb("neg_b", [P, 2, 512], mybir.dt.bfloat16)
        def load_x(t):
            live["x", t] = [SP.did(nc.sync.dma_start(x[:, t, :], x_in[t * P:t * P + P, :]), f"d_x{t}", 16)]
        plan([WHOLE] * 4 + [WHOLE, ON_POOL] * 2 + [ON_POOL, WHOLE])
        load_x(0)
        ident_ready = A.did(nc.scalar.dma_start(ident, const[:, CONST["ident"]]), "d_ident", 16)
        load_gain(ROW1["mix0"])
        small_ready = A.did(nc.scalar.dma_start(sm[:, :], small), "d_small", 16)
        normed_0 = normed_tile(0, 1.0, None, slot2(6))
        prefetch()
        load_x(1)
        prefetch()
        const_ready = A.did(nc.scalar.dma_start(cst[:, P:N_CONST], const[:, P:N_CONST]), "d_const", 16)
        mem_ready = A.did(nc.scalar.dma_start(slot2(4), mem1.rearrange("(t p) d -> p t d", p=P)), "d_mem", 16)
        gates_ready = A.did(nc.scalar.dma_start(par[:, 0:1024], gates), "d_gates", 16)
        pos_i = sb("pos_i", [P, NT], I32)
        pos_ready = A.did(nc.scalar.dma_start(pos_i[:, :], pos), "d_pos", 16)

        def g1(name):
            return sm[:, SMALL[name]]

        ready = tile_to_cols(xT, slot2(6), 0, 0, normed_0, "xT")

        def second_tile():
            ready.update(tile_to_cols(xT, slot2(6), 1, 0, normed_tile(1, 1.0, None, slot2(6)), "xT"))
        XR = arena[:, 0:2, :].rearrange("p a n -> p (a n)")[:, 0:4 * 259].rearrange("p (c n) -> p c n", c=4)
        XC, R, I_, DEC, AA, GATE, GTMP, HS = (arena[:, a, :] for a in (2, 3, 12, 5, 14, 8, 9, 13))

        def quad(ap):
            return ap.rearrange("p (c n) -> p c n", c=4)

        pad_ready = V.did(nc.vector.memset(XR[:, :, 0:3], 0.0))
        xr_toks = []
        for j in range(2):
            tok = up_unit(2 * j, ready, None if j else second_tile)
            xr_toks.append(sum_halves(XR[:, 2 * j:2 * j + 2, 3:259], buf(15, 0), 2 * j, [tok], "sh"))
            live["sh"] = [xr_toks[-1]]
        load_gain(ROW1["mem"])

        mem_rows = []
        for t in range(NT):
            root = norm_begin(t, slot2(4), arena[:, 9, :], 2, [mem_ready])
            mem_rows.append(norm_end(t, slot2(10), slot2(4), 2, root, gain_row, [mem_ready, *live["gain"]]))
        live["gain_read"] = [mem_rows[1][1]]
        load_gain(ROW1["xat0"])
        gate_toks = []
        for j in range(2):
            tok = up_unit(2 * j, ready)
            gate_toks.append(sum_halves(quad(GATE)[:, 2 * j:2 * j + 2, :], buf(15, 0), 2 * j, [tok], "sh"))
            live["sh"] = [gate_toks[-1]]
        conv_toks, sig, y_chunks = [], [], {}

        def recurrence():
            for ch in range(4):
                xc = quad(XC)[:, ch, :]
                cw = g1("conv_w")
                V.after(*xr_toks, pad_ready)
                t0 = V.did(nc.vector.tensor_scalar(xc, XR[:, ch, 0:S], cw[:, ch:ch + 1], g1("conv_b")[:, ch:ch + 1],
                                                   ALU.mult, ALU.add))
                for j in range(1, 4):
                    V.after(t0)
                    t0 = V.did(nc.vector.scalar_tensor_tensor(xc, XR[:, ch, j:j + S], cw[:, 4 * j + ch:4 * j + ch + 1], xc,
                                                              ALU.mult, ALU.add))
                conv_toks.append(t0)
            yield
            lam, ab, ee, zz, z2, acc, neg = g1("lam"), *(rg[:, i, :] for i in range(6))
            V.after(small_ready)
            t0 = V.did(nc.vector.tensor_scalar(neg, lam, -1.0, None, ALU.mult))
            V.after(t0)
            t0 = V.did(nc.vector.tensor_tensor(ab, lam, neg, ALU.max))
            A.after(t0)
            t0 = A.did(nc.scalar.activation(ee, ab, ACT.Exp, scale=-1.0))
            V.after(t0)
            t0 = V.did(nc.vector.tensor_scalar(zz, ee, 2.0, None, ALU.add))
            V.after(t0)
            t0 = V.did(nc.vector.reciprocal(zz, zz))
            V.after(t0)
            t0 = V.did(nc.vector.tensor_tensor(zz, zz, ee, ALU.mult))
            G.after(t0)
            t0 = G.did(nc.gpsimd.tensor_tensor(z2, zz, zz, ALU.mult))
            G.after(t0)
            t0 = G.did(nc.gpsimd.tensor_scalar(acc, z2, 1.0 / 17, 1.0 / 15, ALU.mult, ALU.add))
            for odd in (13, 11, 9, 7, 5, 3, 1):
                G.after(t0)
                t0 = G.did(nc.gpsimd.tensor_tensor(acc, acc, z2, ALU.mult))
                G.after(t0)
                t0 = G.did(nc.gpsimd.tensor_scalar(acc, acc, 1.0 / odd, None, ALU.add))
            G.after(t0)
            t0 = G.did(nc.gpsimd.tensor_tensor(acc, acc, zz, ALU.mult))
            G.after(t0)
            t0 = G.did(nc.gpsimd.tensor_scalar(neg, neg, 0.0, None, ALU.max))
            G.after(t0)
            t0 = G.did(nc.gpsimd.tensor_scalar(acc, acc, 2.0, None, ALU.mult))
            G.after(t0)
            t0 = G.did(nc.gpsimd.tensor_tensor(acc, acc, neg, ALU.add))
            G.after(t0)
            sp4 = rg[:, 6, :]
            decay_ready = G.did(nc.gpsimd.tensor_scalar(sp4, acc, 4.0, None, ALU.mult))

            yield
            gw = par[:, 0:1024].rearrange("p (g n) -> p g n", g=8)
            for g, (dst, bias) in enumerate(((R, "ga_b"), (I_, "gx_b"))):
                for ch in range(4):
                    bank = 2 * g + ch // 2
                    T.after(*conv_toks, gates_ready, *last_of(("bank", bank)))
                    last = nc.tensor.matmul(ps[:, bank, (ch % 2) * S:(ch % 2) * S + S], gw[:, 4 * g + ch, :],
                                            quad(XC)[:, ch, :], start=True, stop=True)
                    if ch % 2:
                        tok = T.did(last)
                        A.after(tok, small_ready, *gate_toks)
                        for c2 in (ch - 1, ch):
                            s_ = A.did(nc.scalar.activation(quad(dst)[:, c2, :], ps[:, bank, (c2 % 2) * S:(c2 % 2) * S + S],
                                                            ACT.Sigmoid, bias=g1(bias)[:, c2:c2 + 1]))
                        live["bank", bank] = [s_]
                        sig.append(s_)

            yield
            A.after(decay_ready, *sig)
            for ch in range(4):
                th = A.did(nc.scalar.activation(quad(R)[:, ch, :], quad(R)[:, ch, :], ACT.Tanh, scale=sp4[:, ch:ch + 1]))
            V.after(th)
            t0 = V.did(nc.vector.tensor_scalar(DEC, R, 1.0, None, ALU.add))
            V.after(t0)
            for hs in (slice(0, 512), slice(512, 1024)):
                t0 = V.did(nc.vector.reciprocal(DEC[:, hs], DEC[:, hs]))
                yield
            V.after(t0)
            t0 = V.did(nc.vector.scalar_tensor_tensor(R, R, 2.0, DEC, ALU.mult, ALU.mult))
            V.after(t0)
            yield
            a_tok = V.did(nc.vector.tensor_scalar(AA, R, -1.0, 1.0, ALU.mult, ALU.add))
            V.after(a_tok)
            t0 = V.did(nc.vector.scalar_tensor_tensor(R, AA, 1.0, R, ALU.add, ALU.mult))
            yield
            A.after(t0)
            root = A.did(nc.scalar.activation(R, R, ACT.Sqrt))
            yield
            G.after(*sig, *conv_toks)
            t1 = G.did(nc.gpsimd.tensor_tensor(I_, I_, XC, ALU.mult))
            V.after(t1, root)
            t0 = V.did(nc.vector.tensor_tensor(I_, I_, R, ALU.mult))
            V.after(t0)
            yield
            for ch in range(4):
                t0 = V.did(nc.vector.tensor_tensor_scan(quad(HS)[:, ch, :], quad(AA)[:, ch, :], quad(I_)[:, ch, :], 0.0,
                                                        ALU.mult, ALU.add))
            V.after(t0, *gelu)
            yb_tok = V.did(nc.vector.scalar_tensor_tensor(GATE, HS, 0.5, GATE, ALU.mult, ALU.mult))
            while not live.get("xT"):
                yield
            tok = split(xT[:, 4:8, 0, :], xT[:, 4:8, 1, :], quad(GATE), [yb_tok, *live["xT"]])
            y_chunks.update({("chunk", k): tok for k in range(4, 8)})


        gelu = []

        def gate_branch():
            A.after(*gate_toks)
            g2 = A.did(nc.scalar.activation(GTMP, GATE, ACT.Square))
            V.after(g2)
            t1 = V.did(nc.vector.tensor_scalar(GTMP, GTMP, 0.044715, 1.0, ALU.mult, ALU.add))
            G.after(t1)
            t1 = G.did(nc.gpsimd.tensor_tensor(GTMP, GTMP, GATE, ALU.mult))
            yield
            yield
            A.after(t1)
            t1 = A.did(nc.scalar.activation(GTMP, GTMP, ACT.Tanh, scale=float(np.sqrt(2 / np.pi))))
            yield
            V.after(t1)
            gelu.append(V.did(nc.vector.scalar_tensor_tensor(GATE, GTMP, 1.0, GATE, ALU.add, ALU.mult)))

        in_background(recurrence())
        in_background(gate_branch())
        V.after(small_ready)
        for name, width in (("ev_q", P), ("xq0", 256), ("xq1", 256)):
            gains_ready = V.did(nc.vector.tensor_scalar(g1(name), g1(name), float(width) ** -0.5, None, ALU.mult))
        V.after(const_ready, ident_ready)
        for dst, src in ((ident_b[:, :], ident), (neg_b[:, 0, :], c("neg1")), (neg_b[:, 1, :], c("neg2"))):
            mask_ready = V.did(nc.vector.tensor_copy(dst, src))

        ROWS, KT, QT, VB = slot2(10), quad(arena[:, 4, :]), quad(arena[:, 6, :]), arena[:, 7, :]
        qk_ends = project(4, xT, 2, 512, 2, ready)
        memory = {}
        for t in range(NT):
            memory.update(tile_to_cols(memT, slot2(10), t, 0, mem_rows[t], "memT"))
        rows_tok = head_norms([(ROWS[:, t, :], ps[:, 4 + 2 * t:6 + 2 * t, :].rearrange("p a n -> p (a n)"),
                                arena[:, (15, 13)[t], :], qk_ends[t], [4 + 2 * t, 5 + 2 * t]) for t in range(NT)],
                              8, P, 16, [*memory.values(), *live["sh"]])
        paused, background[:] = list(background), []
        v_ends = project(0, xT, 1, 512, 4, ready)
        live["xT"] = [v_ends[1]]
        for t in range(NT):
            A.after(v_ends[1])
            vt = A.did(nc.scalar.activation(VB[:, t * 512:t * 512 + 512], ps[:, t, :], ACT.Copy))
            live["bank", t] = [vt]
        V.after(gains_ready)
        q_tok = rows_to_cols(QT, [ROWS[:, t, 0:512] for t in range(NT)], 4, g1("ev_q"), lambda t: 4 + t, rows_tok)
        k_tok = rows_to_cols(KT, [ROWS[:, t, 512:1024] for t in range(NT)], 4, g1("ev_k"), lambda t: 6 + t, rows_tok)
        heads = [dict(q=[QT[:, h, :]], k=[KT[:, h, :]], neg=neg_b[:, 0, :], cnt=c("cnt"),
                      v=lambda mm, cc, h=h: VB[:, mm * 512 + h * P:mm * 512 + h * P + P],
                      place=[(0, P, (h % 2) * S)], bank=h // 2, open=(h % 2 == 0),
                      close=(slice(h - 1, h + 1), 2) if h % 2 else None) for h in range(4)]
        background[:] = paused
        o = attention(heads, arena[:, 0, :], arena[:, 1, :], [*q_tok, *k_tok, vt], 40, "at0", 4)
        product = project_late_tile(4, xT, o, list(range(KC)), y_chunks)

        def head_cols(dst, rows, toks, gain, bank):
            g = []
            for t in range(NT):
                tr = transpose_rows(rows[:, t, :], t, 8, bank + 2 * t, [toks[t]])
                for b in range(2):
                    pv = ps[:, bank + 2 * t + b, :].rearrange("p (k n) -> p k n", k=4)
                    V.after(tr[b], gains_ready)
                    tok = V.did(nc.vector.tensor_tensor(dst[:, 4 * b:4 * b + 4, t * P:t * P + P], pv,
                                                        g1(gain).unsqueeze(2).broadcast_to([P, 4, P]), ALU.mult))
                    live["bank", bank + 2 * t + b] = [tok]
                    g.append(tok)
            return g

        def head_rows(dst, bank, ends, st0, wait):
            return head_norms([(dst[:, t, :], ps[:, bank + 2 * t:bank + 2 * t + 2, :].rearrange("p a n -> p (a n)"),
                                arena[:, (9, 15)[t], :], ends[t], [bank + 2 * t, bank + 2 * t + 1])
                               for t in range(NT)], 4, 256, st0, wait)

        KR, KTX, QTX, VX = slot2(10), slot2(0), slot2(2), slot2(4)
        KT8, QT8 = (b.rearrange("p a n -> p (a n)").rearrange("p (k n) -> p k n", k=8) for b in (KTX, QTX))

        def x_to_cols(normed, bank):
            ready = {}
            for t in range(NT):
                ready.update(tile_to_cols(xT, slot2(6), t, bank, normed[t], "xT"))
            return ready

        def queries(layer, ready, base, v_base, v_from):
            q_ends = project(base, xT, 2, 512, 2, ready)
            live["xT"] = [q_ends[1]]
            q_rows = head_rows(slot2(6), base, q_ends, 24, [])
            v_ends = project(v_base, memT, 2, 512, 2, memory, (v_from, KC))
            live["memT"] = [v_ends[1]]
            q_cols = head_cols(QT8, slot2(6), q_rows, f"xq{layer}", base)
            A.after(v_ends[1])
            for t in range(NT):
                src = ps[:, v_base + 2 * t:v_base + 2 * t + 2, :].rearrange("p a n -> p (a n)")
                vv = A.did(nc.scalar.activation(VX[:, t, :], src, ACT.Copy))
                live["bank", v_base + 2 * t] = live["bank", v_base + 2 * t + 1] = [vv]
            return [*q_cols, vv]

        def attend(layer, wait, base):
            heads = [dict(q=[QT8[:, 2 * h + cc, :] for cc in range(2)], k=[KT8[:, 2 * h + cc, :] for cc in range(2)],
                          v=lambda mm, cc, h=h: VX[:, mm, h * 256 + cc * P:h * 256 + cc * P + P],
                          place=[(0, P, 0), (0, P, S)], bank=h % 2, open=True,
                          close=(slice(2 * h, 2 * h + 2), 2)) for h in range(4)]
            o = attention(heads, arena[:, 12, :], arena[:, 13, :], wait, 40, "xa", base)
            return project_late_tile(4, xT, o, list(range(KC)))

        normed = [product[2]]
        project(0, memT, 2, 512, 2, memory, (0, 2))
        normed.append(normed_tile(1, 1.0, product, slot2(6)))
        load_gain(ROW1["mlp0"])
        k_ends = project(0, memT, 2, 512, 2, memory, (2, KC))
        ready = x_to_cols(normed, 4)
        k_rows = head_rows(KR, 0, k_ends, 16, all_x())
        project(4, memT, 2, 512, 2, memory, (0, 4))
        k_cols = head_cols(KT8, KR, k_rows, "xk0", 0)
        q_cols = queries(0, ready, 0, 4, 4)
        product = attend(0, [*k_cols, *q_cols], 0)
        def rotary_tables():
            MAGIC = 1.5 * 2.0 ** 23
            C1 = 6.28125
            C2 = float(np.float32(2 * np.pi - C1))
            C2 = float(np.float32(np.round(C2 * 2 ** 21) / 2 ** 21))
            C3 = float(2 * np.pi - C1 - C2)
            posf, ang, kk, red = stat[:, 80:82], arena[:, 9, 0:64], arena[:, 9, 64:128], arena[:, 9, 128:192]
            V.after(pos_ready, *last_of("mix_end"))
            t0 = V.did(nc.vector.tensor_copy(posf, pos_i[:, :]))
            V.after(t0, const_ready)
            for t in range(NT):
                t0 = V.did(nc.vector.tensor_scalar(ang[:, 32 * t:32 * t + 32], c("freq"), posf[:, t:t + 1], None, ALU.mult))
            for i, (shift, phase) in enumerate(((0.25, np.pi / 2), (0.0, 0.0))):
                V.after(t0)
                t0 = V.did(nc.vector.tensor_scalar(kk, ang, float(1 / (2 * np.pi)), shift, ALU.mult, ALU.add))
                V.after(t0)
                t0 = V.did(nc.vector.tensor_scalar(kk, kk, MAGIC, None, ALU.add))
                V.after(t0)
                t0 = V.did(nc.vector.tensor_scalar(kk, kk, -MAGIC, None, ALU.add))
                V.after(t0)
                t0 = V.did(nc.vector.scalar_tensor_tensor(red, kk, -C1, ang, ALU.mult, ALU.add))
                for cc in (C2, C3):
                    V.after(t0)
                    t0 = V.did(nc.vector.scalar_tensor_tensor(red, kk, -cc, red, ALU.mult, ALU.add))
                V.after(t0)
                t0 = V.did(nc.vector.tensor_scalar(red, red, float(phase), float(np.float32(3.1415925)), ALU.add, ALU.min))
                V.after(t0)
                t0 = V.did(nc.vector.tensor_scalar(red, red, -3.1415925, None, ALU.max))
                yield
                A.after(t0)
                t0 = A.did(nc.scalar.activation(trig[:, i, :, :].rearrange("p a n -> p (a n)"), red, ACT.Sin))
            live["rope"] = [t0]
            yield
        rotary = rotary_tables()
        product = feed_forward(1.0, product, D_FF, up_relu2, 3, ROW1["xat1"], beside=lambda: next(rotary),
                               before_last=lambda: next(rotary))
        next(rotary)
        trig_ready = live["rope"][0]

        AM = slot2(4).rearrange("p a n -> p (a n)").rearrange("p (s g n) -> p s g n", s=2, g=4)
        A.after(product[1][0], *last_of(("h", 0)))
        pool_ready = A.did(nc.scalar.dma_start(slot2(4), pool_mat.rearrange("p (a n) -> p a n", a=2)), "d_pool", 16)
        pool_ready = A.did(nc.scalar.dma_start(arena[:, 14, :], scale_row), "d_pool", 16)
        normed = normed_pair(1.0, product, slot2(6), False)
        k_ends = project(0, memT, 2, 512, 2, memory)
        d_toks = []
        for kc in range(KC):
            bank, off, g = 4 + kc // 2, (kc % 2) * S, kc // 2
            T.after(pool_ready, normed[0][kc // 4], normed[1][kc // 4], *last_of(("bank", bank)))
            nc.tensor.matmul(ps[:, bank, off:off + S], slot2(6)[:, 0, kc * P:kc * P + P], AM[:, 0, g, :], start=True,
                             stop=False)
            last = nc.tensor.matmul(ps[:, bank, off + P:off + S], slot2(6)[:, 1, kc * P:kc * P + P], AM[:, 1, g, P:S],
                                    start=False, stop=True)
            if kc % 2:
                tok = T.did(last)
                d_toks.append(evac_cols(xT, slice(kc - 1, kc + 1), slice(0, S), bank, S, g1("mix_g1")[:, kc - 1:kc + 1],
                                        slot2(12)[:, g // 2, (g % 2) * 512:(g % 2) * 512 + 512], [tok], "xT"))
        k_rows = head_rows(KR, 0, k_ends, 16, all_x())
        s = take()
        for g in range(4):
            for t in range(NT):
                bank, off = 4 + 2 * t + g // 2, (g % 2) * S
                T.after(*d_toks, *last_of(("bank", bank)))
                for j in range(2):
                    h, l = xT[:, 2 * g + j, 0, :], xT[:, 2 * g + j, 1, :]
                    cs, ts = slice((2 * g + j) * S, (2 * g + j) * S + S), slice(t * P, t * P + P)
                    o = ps[:, bank, off:off + S]
                    nc.tensor.matmul(o, h[:, ts], w_hi[:, s, cs], start=(j == 0), stop=False)
                    nc.tensor.matmul(o, h[:, ts], w_lo[:, s, cs], start=False, stop=False)
                    last = nc.tensor.matmul(o, l[:, ts], w_hi[:, s, cs], start=False, stop=(j == 1))
        tok = release(s, last)
        live["xT"] = [tok]
        k_cols = head_cols(KT8, KR, k_rows, "xk1", 0)
        normed = []
        for t in range(NT):
            toks = []
            for h in range(2):
                bank, tmp = 4 + 2 * t + h, slot2(12)[:, t, h * 512:h * 512 + 512]
                V.after(tok, pool_ready)
                m_ = V.did(nc.vector.tensor_tensor(tmp, ps[:, bank, :], arena[:, 14, h * 512:h * 512 + 512], ALU.mult))
                live["bank", bank] = [m_]
                xs = x[:, t, h * 512:h * 512 + 512]
                V.after(m_)
                toks.append(V.did(nc.vector.tensor_tensor(xs, xs, tmp, ALU.add)))
            live["x", t] = toks
            normed.append(normed_tile(t, 1.0, None, slot2(6)))
            if t == 0:
                project(0, memT, 2, 512, 2, memory, (0, 2))
        load_gain(ROW1["mlp1"])

        project(0, memT, 2, 512, 2, memory, (2, 6))
        ready = x_to_cols(normed, 4)
        q_cols = queries(1, ready, 4, 0, 6)
        product = attend(1, [*k_cols, *q_cols], 4)
        MR, MN = slot2(12), slot2(10)

        def load_memory(row):
            src = gain_source(row)
            A.after(*last_of("mix_end"), *last_of("mem_cols"))
            live["mem_in"] = [A.did(nc.scalar.dma_start(MR, mem2.rearrange("(t p) d -> p t d", p=P)), "d_mem2", 16),
                              A.did(nc.scalar.dma_start(arena[:, 14, :], src), "d_mgain", 16)]

        def memory_roots():
            live["mem_root"] = [norm_begin(t, MR, arena[:, 9, :], 2, [*live["mem_in"], *last_of("mix_end")])
                                for t in range(NT)]

        def memory_cols():
            rows = [norm_end(t, MN, MR, 2, live["mem_root"][t], arena[:, 14, :],
                             [*live["mem_in"], *last_of("mix_end")]) for t in range(NT)]
            done = []
            for t in range(NT):
                done += tile_to_cols(memT, MN, t, 0, rows[t], "memT").values()
            live["mem_cols"] = done
        load_memory(FIRST2 + ROW2["mem"])
        product = feed_forward(1.0, product, D_FF, up_relu2, 3, FIRST2 + ROW2["ffn1"], beside=memory_roots, before_last=memory_cols)
        for t in range(NT):
            add_rows(t, 1.0, product)

        def lp(name, n=None):
            return par[:, LAYER[name]]

        def layer():
            lid = prog.n_loops - 1
            row = prog.vars[lid] * len(GAINS2) + FIRST2
            which = nc.scalar.snap(prog.vars[lid] + 0)
            A.after(*last_of("par"))
            par_ready = A.did(nc.scalar.dma_start(par[:, 0:N_LAYER], layer_par[bass.ds(which, 1), :, :]
                                                  .rearrange("a p n -> (a p) n")), "d_par", 16)
            T.after(*live["mem_cols"])
            MV, MKT = (arena[:, 15, h:h + 512].rearrange("p (a n) -> p a n", a=2) for h in (0, 512))
            MKR = arena[:, 9, 512:1024].rearrange("p (t n) -> p t n", t=NT)
            mk_ends = project(2, memT, 1, 256, KC, None)
            mk_rows, mk_cols = [], []

            def key_rows():
                mk_rows.extend(head_norms([(MKR[:, t, :], ps[:, 2 + t, 0:256], arena[:, 9, 256 * t:256 * t + 256],
                                            mk_ends[t], [2 + t]) for t in range(NT)], 4, 64, 60, last_of("mem_cols")))

            def key_cols():
                V.after(par_ready)
                mk_cols.extend(rows_to_cols(MKT, [MKR[:, t, :] for t in range(NT)], 2, lp("mk_g"), lambda t: t, mk_rows))
            product = feed_forward(0.5, None, D_FF2, up_swiglu, 2, row + ROW2["mix"], 4, tile_done=key_rows,
                                   before_last=key_cols)

            normed = normed_pair(0.5, product, slot2(6))
            load_gain(row + ROW2["ffn2"])
            plan([WHOLE] * 6 + [NARROW] * 4)
            m_ends = project(0, memT, 1, 256, KC, None)
            live["memT"] = [m_ends[1]]
            x_cols = x_to_cols(normed, 4)
            A.after(m_ends[1])
            for t in range(NT):
                mv_copy = A.did(nc.scalar.activation(MV[:, t, :], ps[:, t, 0:256], ACT.Copy))
                live["bank", t] = [mv_copy]

            V.after(par_ready)
            V.did(nc.vector.tensor_scalar(lp("qk_g")[:, 0:384], lp("qk_g")[:, 0:384], 64 ** -0.5, None, ALU.mult))
            scaled = V.did(nc.vector.tensor_scalar(lp("mq_g"), lp("mq_g"), 64 ** -0.5, None, ALU.mult))
            QR = slot2(0)
            VW = arena[:, 4, 0:256].rearrange("p (t n) -> p t n", t=NT)
            cosb, sinb = (trig[:, i, :, :].unsqueeze(2).broadcast_to([P, NT, 8, 32]) for i in range(2))
            qv = QR[:, :, 0:512].rearrange("p t (h c) -> p t h c", c=64)
            x1, x2 = qv[:, :, :, 0:32], qv[:, :, :, 32:64]
            r1, r2, r3 = (a.rearrange("p (t h c) -> p t h c", t=NT, c=32)
                          for a in (arena[:, 13, 0:512], arena[:, 13, 512:1024], arena[:, 14, 0:512]))
            QKT = slot2(2).rearrange("p a n -> p (a n)")[:, 0:1536].rearrange("p (k n) -> p k n", k=6)
            rotated = []

            def window_rows():
                toks = head_norms([(QR[:, t, 0:512], ps[:, 4 + t, :], arena[:, 8, 512 * t:512 * t + 512], qk_ends[t],
                                    [4 + t]) for t in range(NT)], 8, 64, 16, [scaled, trig_ready], lp("qk_g"))
                yield
                V.after(*toks)
                r = [V.did(nc.vector.tensor_tensor(r1, x1, sinb, ALU.mult))]
                r.append(V.did(nc.vector.tensor_tensor(r2, x2, sinb, ALU.mult)))
                V.after(*r)
                r = [V.did(nc.vector.tensor_tensor(r3, x1, cosb, ALU.mult))]
                r.append(V.did(nc.vector.tensor_tensor(x2, x2, cosb, ALU.mult)))
                V.after(*r)
                rotated.extend([V.did(nc.vector.tensor_tensor(x1, r3, r2, ALU.subtract)),
                                V.did(nc.vector.tensor_tensor(x2, x2, r1, ALU.add))])
                yield
            qk_ends = project(4, xT, 1, 512, 4, x_cols)
            chain = window_rows()
            next(chain)
            in_background(chain)

            Z6 = arena[:, 9:11, :].rearrange("p a n -> p (a n)")[:, 0:1536].rearrange("p (k n) -> p k n", k=6)
            YP = arena[:, 11, 0:3 * 286].rearrange("p (k n) -> p k n", k=3)
            YC = arena[:, 12, 0:768].rearrange("p (k n) -> p k n", k=3)
            pad = V.did(nc.vector.memset(YP[:, :, 0:30], 0.0))
            zt = []
            for j, bank in enumerate((2, 0, 2)):
                tok = up_unit(bank, x_cols)
                zt.append(sum_halves(Z6[:, 2 * j:2 * j + 2, :], arena[:, 5, 0:512].rearrange("p (k n) -> p k n", k=2),
                                     bank, [tok], "sh"))
                live["sh"] = [zt[-1]]
            A.after(*zt)
            sg = A.did(nc.scalar.activation(Z6[:, 3:6, :], Z6[:, 3:6, :], ACT.Sigmoid))
            V.after(sg, *zt, pad)
            glu = V.did(nc.vector.tensor_tensor(YP[:, :, 30:286], Z6[:, 0:3, :], Z6[:, 3:6, :], ALU.mult))

            cw, conv_last = lp("conv_w"), {}

            def tap(j, ch):
                if j == 0:
                    V.after(glu, par_ready)
                    conv_last[ch] = V.did(nc.vector.tensor_scalar(YC[:, ch, :], YP[:, ch, 0:S], cw[:, ch:ch + 1],
                                                                  lp("conv_b")[:, ch:ch + 1], ALU.mult, ALU.add))
                else:
                    V.after(conv_last[ch])
                    conv_last[ch] = V.did(nc.vector.scalar_tensor_tensor(
                        YC[:, ch, :], YP[:, ch, j:j + S], cw[:, 3 * j + ch:3 * j + ch + 1], YC[:, ch, :],
                        ALU.mult, ALU.add))
            taps = [(j, ch) for j in range(31) for ch in range(2)]

            terms = [(a, o) for a in (5, 6) for o in (512, 768)]
            free = [None] * len(terms)
            others = list(range(31))

            def run_other_taps(n):
                batch = [others.pop(0) for _ in range(min(n, len(others)))]
                made = []
                for j in batch:
                    a, o = terms[j % 4]
                    A.after(glu, par_ready, *([free[j % 4]] if free[j % 4] else []))
                    made.append(A.did(nc.scalar.activation(arena[:, a, o:o + S], YP[:, 2, j:j + S], ACT.Copy,
                                                           scale=cw[:, 3 * j + 2:3 * j + 3])))
                for j, m in zip(batch, made):
                    a, o = terms[j % 4]
                    G.after(m, *([conv_last[2]] if j else []))
                    before = YC[:, 2, :] if j else lp("conv_b")[:, 2:3].broadcast_to([P, S])
                    free[j % 4] = conv_last[2] = G.did(nc.gpsimd.tensor_tensor(YC[:, 2, :], arena[:, a, o:o + S],
                                                                               before, ALU.add))

            def run_taps(n):
                for _ in range(min(n, len(taps))):
                    tap(*taps.pop(0))

            finish_background()
            qk_cols = rows_to_cols(QKT, [QR[:, t, 0:512] for t in range(NT)], 4, None, lambda t: t, [rotated[-1]] * NT)
            for k in range(0, KC, 2):
                mv_ends = rows_unit(6, [chunk(xT, k + j, x_cols) for j in range(2)], 1, 384, k == 0, k == 6)
                run_taps(5)
                run_other_taps(4)
            live["xT"] = [mv_ends[1]]
            mq_ready, vw_ready = [], []

            def memory_queries():
                for t in range(NT):
                    A.after(mv_ends[1])
                    vt = A.did(nc.scalar.activation(VW[:, t, :], ps[:, 6 + t, 256:384], ACT.Copy))
                vw_ready.append(vt)
                mq_rows = head_norms([(QR[:, t, 512:768], ps[:, 6 + t, 0:256], arena[:, 14, 512 + 256 * t:768 + 256 * t],
                                       vt, [6 + t]) for t in range(NT)], 4, 64, 32, [])
                yield
                for t in range(NT):
                    T.after(mq_rows[t], *last_of(("bank", 3)))
                    for j in range(2):
                        last = nc.tensor.transpose(ps[:, 3, (2 * t + j) * P:(2 * t + j + 1) * P],
                                                   QR[:, t, 512 + j * P:512 + (j + 1) * P], ident)
                V.after(T.did(last))
                for j in range(2):
                    pv = ps[:, 3, :].rearrange("p (t k n) -> p t k n", t=NT, k=2)[:, :, j, :]
                    tok = V.did(nc.vector.tensor_scalar(QKT[:, 4 + j, :].rearrange("p (t n) -> p t n", t=NT), pv,
                                                        lp("mq_g")[:, j:j + 1], None, ALU.mult))
                live["bank", 3] = [tok]
                mq_ready.append(tok)
                yield

            MU, LT, VR = arena[:, 13, 0:256], arena[:, 14, 0:768].rearrange("p (k n) -> p k n", k=3), arena[:, 13, 256:512]
            y_conv = {}

            def channel_sum(src, after):
                T.after(*after, *last_of(("bank", 3)))
                for k in range(3):
                    last = nc.tensor.matmul(ps[:, 3, 0:S], c("ones"), src[:, k, :], start=(k == 0), stop=(k == 2))
                return T.did(last)

            def conv_norm():
                while taps:
                    run_taps(6)
                    run_other_taps(3)
                    yield
                tok = channel_sum(YC, conv_last.values())
                A.after(tok)
                t0 = A.did(nc.scalar.activation(MU, ps[:, 3, 0:S], ACT.Copy, scale=1.0 / 384))
                live["bank", 3] = [t0]
                V.after(t0)
                t0 = V.did(nc.vector.tensor_tensor(YC, YC, MU.unsqueeze(1).broadcast_to([P, 3, S]), ALU.subtract))
                A.after(t0)
                sq = A.did(nc.scalar.activation(LT, YC, ACT.Square))
                yield
                tok = channel_sum(LT, [sq])
                V.after(tok)
                t1 = V.did(nc.vector.tensor_scalar(VR, ps[:, 3, 0:S], 1.0 / 384, EPS, ALU.mult, ALU.add))
                live["bank", 3] = [t1]
                V.after(t1)
                t1 = V.did(nc.vector.reciprocal(VR, VR))
                yield
                A.after(t1)
                t1 = A.did(nc.scalar.activation(VR, VR, ACT.Sqrt))
                V.after(t1)
                t1 = V.did(nc.vector.tensor_tensor(YC, YC, VR.unsqueeze(1).broadcast_to([P, 3, S]), ALU.mult))
                V.after(t1)
                for k in range(3):
                    t1 = V.did(nc.vector.tensor_scalar(YC[:, k, :], YC[:, k, :], lp("ln_g")[:, k:k + 1],
                                                       lp("ln_b")[:, k:k + 1], ALU.mult, ALU.add))
                yield
                A.after(t1)
                t2 = A.did(nc.scalar.activation(LT, YC, ACT.Sigmoid))
                V.after(t2)
                t2 = V.did(nc.vector.tensor_tensor(YC, YC, LT, ALU.mult))
                live["par"] = [t2]
                y_tok = split(xT[:, 0:3, 0, :], xT[:, 0:3, 1, :], YC, [t2, *last_of("xT")])
                y_conv.update({("chunk", k): y_tok for k in range(3)})
            in_background(memory_queries())
            in_background(conv_norm())

            heads = []
            for j in range(3):
                for side in range(2):
                    ss = slice(64 * side, 64 * side + 64)
                    heads.append(dict(q=[QKT[ss, j, :]], k=[QKT[ss, 3, :]], neg=neg_b[:, 1, :], v_wait=vw_ready,
                                      sink=lp("sinks")[:, 2 * j + side:2 * j + side + 1],
                                      v=lambda mm, cc, ss=ss: VW[:, mm, ss], place=[(64 * side, 64 * side + 64, 0)],
                                      bank=j % 2, open=(side == 0), close=(slice(3 + j, 4 + j), 1) if side else None))
            for j in range(2):
                for side in range(2):
                    ss = slice(64 * side, 64 * side + 64)
                    vs = slice(128 * j + 64 * side, 128 * j + 64 * side + 64)
                    heads.append(dict(q=[QKT[ss, 4 + j, :]], k=[MKT[ss, j, :]], wait=mq_ready,
                                      v=lambda mm, cc, vs=vs: MV[:, mm, vs], place=[(64 * side, 64 * side + 64, 0)],
                                      bank=(j + 1) % 2, open=(side == 0),
                                      close=(slice(6 + j, 7 + j), 1) if side else None))
            o = attention(heads, arena[:, 7, :], arena[:, 8, :], [*qk_cols, *mk_cols, mv_copy], 40, "sw", 0, 3)
            
            order = [4, 5, 6, 7, 3, 0, 1, 2]
            product = project_late_tile(4, xT, o, order, y_conv)

            load_memory(row + len(GAINS2) + ROW2["mem"])
            product = feed_forward(1.0, product, D_FF2, up_swiglu, 2, row + ROW2["final"], beside=memory_roots,
                                   before_last=memory_cols)

            live["x", 0], live["x", 1] = normed_pair(0.5, product, x)
            load_gain(row + len(GAINS2))

        live["par"] = [gates_ready, ("pe", prog.counts["pe"])]
        prog.loop(2, layer)

        for t in range(NT):
            SP.after(*live["x", t])
            done = SP.did(nc.sync.dma_start(out[t * P:t * P + P, :], x[:, t, :]), "d_out", 16)
        SP.after(done, *live["gain"])


def _up_units(w):
    n = w.shape[1] // 256
    return w.reshape(KC, P, n, 256).transpose(2, 1, 0, 3).reshape(n, P, UNIT)


def _down_units(w, cols=1024):
    j = UNIT // cols
    n = w.shape[0] // (P * j)
    return w.reshape(n, j, P, cols).transpose(0, 2, 1, 3).reshape(n, P, UNIT)


def _narrow_units(w):
    u = np.zeros((4, P, UNIT), w.dtype)
    u[:, :, 0:PARTIAL] = w.reshape(4, 2, P, 384).transpose(0, 2, 1, 3).reshape(4, P, PARTIAL)
    return u


def _gated_units(w1, w3, w2):
    ups = [_up_units(w) for w in ((w1, w3) if w3 is not None else (w1,))]
    dn = _down_units(w2)
    n = dn.shape[0]
    out = [u[0] for u in ups]
    for s in range(n):
        if s + 1 < n:
            out += [u[s + 1] for u in ups]
        out.append(dn[s])
    return np.stack(out)


def _chunks(v):
    return v.reshape(-1, P).T


def _layout(i):
    w_in, units = i["ev_w_in"][0], []
    w_out = i["ev_w_out"][0]
    units += [_up_units(w_in[:, 1536:2048]), _up_units(w_in[:, 2048:2560]), _down_units(w_in[:, 0:1024]),
              _down_units(w_in[:, 1024:1536], 512), _down_units(w_out)]
    for l in range(2):
        kv = i["xa_w_kv"][l]
        units.append(_down_units(kv[:, 0:1024]))
        if l == 1:
            units.append(i["od_pool_w"][0].reshape(4, 2, P, 256).transpose(2, 0, 1, 3).reshape(1, P, UNIT))
        values = _down_units(kv[:, 1024:2048])
        units += [values[0:2 + l], _down_units(i["xa_w_q"][l]), values[2 + l:4], _down_units(i["xa_w_o"][l]),
                  _gated_units(i["mlp_w1"][l], None, i["mlp_w2"][l])]
    order = [0, 3, 1, 4, 2, 5]
    for l in range(2):
        w = i["w_in_2"][l]
        q = w[:, 768:1152].reshape(D, 6, 64)[:, order].reshape(D, 384)
        qk = np.concatenate([q, w[:, 1152:1280]], 1)
        mv = np.concatenate([w[:, 1408:1664], w[:, 1280:1408]], 1)
        wo = i["w_out_2"][l]
        wo = np.concatenate([wo[0:384], wo[384:768].reshape(6, 64, D)[order].reshape(384, D), wo[768:]], 0)
        wo = wo.reshape(KC, P, D)[[4, 5, 6, 7, 3, 0, 1, 2]].reshape(D, D)
        mem_kv = _up_units(i["w_mem_kv_2"][l])
        units += [mem_kv[0:1], _gated_units(i["ffn1_w1_2"][l], i["ffn1_w3_2"][l], i["ffn1_w2_2"][l]),
                  mem_kv[1:2], _down_units(qk, 512), _up_units(w[:, 0:768]),
                  _narrow_units(mv), _down_units(wo),
                  _gated_units(i["ffn2_w1_2"][l], i["ffn2_w3_2"][l], i["ffn2_w2_2"][l])]
    units.append(np.zeros((AHEAD, P, UNIT), np.float32))
    weights = np.concatenate(units, 0)

    small = np.zeros((P, N_SMALL), np.float32)
    def put(dst, table, name, v):
        dst[:, table[name]] = v
    put(small, SMALL, "mix_g1", _chunks(i["mix_norm_g"][1]))
    for l in range(2):
        put(small, SMALL, f"xq{l}", np.tile(_chunks(i["xa_q_norm_g"][l]), (1, 2)))
        put(small, SMALL, f"xk{l}", np.tile(_chunks(i["xa_k_norm_g"][l]), (1, 2)))
    put(small, SMALL, "ev_q", np.tile(_chunks(i["ev_q_norm_g"][0]), (1, 4)))
    put(small, SMALL, "ev_k", np.tile(_chunks(i["ev_k_norm_g"][0]), (1, 4)))
    put(small, SMALL, "conv_w", i["ev_conv_w"][0].reshape(4, 4, P).transpose(2, 0, 1).reshape(P, 16))
    put(small, SMALL, "conv_b", _chunks(i["ev_conv_b"][0]))
    put(small, SMALL, "ga_b", _chunks(i["ev_gate_a_b"][0]))
    put(small, SMALL, "gx_b", _chunks(i["ev_gate_x_b"][0]))
    put(small, SMALL, "lam", _chunks(i["ev_lambda"][0]))
    gates = np.concatenate([i["ev_gate_a_w"][0], i["ev_gate_x_w"][0]], 0).transpose(1, 0, 2).reshape(P, 1024)

    layers = np.zeros((2, P, N_LAYER), np.float32)
    for l in range(2):
        d = layers[l]
        put(d, LAYER, "conv_w", i["conv_w_2"][l].reshape(31, 3, P).transpose(2, 0, 1).reshape(P, 93))
        put(d, LAYER, "conv_b", _chunks(i["conv_b_2"][l]))
        put(d, LAYER, "ln_g", _chunks(i["conv_ln_g_2"][l]))
        put(d, LAYER, "ln_b", _chunks(i["conv_ln_b_2"][l]))
        put(d, LAYER, "sinks", i["swa_sinks_2"][l][order])
        put(d, LAYER, "mq_g", np.tile(i["mem_q_norm_2"][l], 2)[:, None])
        put(d, LAYER, "mk_g", np.tile(i["mem_k_norm_2"][l], 2)[:, None])
        put(d, LAYER, "qk_g", np.concatenate([np.tile(i["swa_q_norm_2"][l], 6), np.tile(i["swa_k_norm_2"][l], 2)]))

    gains = np.stack([i["mix_norm_g"][0], i["mem_norm_g"], i["xattn_norm_g"][0], i["mlp_norm_g"][0],
                      i["xattn_norm_g"][1], i["mlp_norm_g"][1],
                      *(i[f"{name}_norm_2"][l] for l in range(2) for name in GAINS2),
                      *np.zeros((2, D), np.float32)])

    qi, kj = np.arange(S)[:, None], np.arange(S)[None, :]
    def masked(m):
        return np.where(m, 0.0, BIG).astype(np.float32).reshape(NT, P, S).transpose(1, 0, 2).reshape(P, 512)
    near = (qi >= kj) & (qi - kj <= 128)
    by4, by16 = ((qi >= kj) & ((qi - kj) % r == 0) for r in (4, 16))
    cnt = (near.astype(np.float32) + by4 + by16).astype(np.float32)
    const = np.zeros((P, N_CONST), np.float32)
    put(const, CONST, "ident", np.eye(P))
    put(const, CONST, "ones", 1.0)
    put(const, CONST, "neg1", masked(cnt > 0))
    put(const, CONST, "cnt", cnt.reshape(NT, P, S).transpose(1, 0, 2).reshape(P, 512))
    put(const, CONST, "neg2", masked((qi >= kj) & (qi - kj < 128)))
    freq = np.float32(10000.0) ** (-np.arange(0, 64, 2, dtype=np.float32) / np.float32(64))
    put(const, CONST, "freq", freq)
    tt, ss = np.arange(S)[None, :], np.arange(S)[:, None]
    pool = np.zeros((S, 4, S), np.float32)
    for g, w in enumerate((2, 4, 8, 16)):
        inside = (ss <= tt) & (ss > tt - w)
        pool[:, g, :] = inside / np.minimum(tt + 1, w) - (ss == tt)
    pool = pool.reshape(NT, P, 4, S).transpose(1, 0, 2, 3).reshape(P, 2048)
    return {
        "weights": weights, "small": small, "const": const, "layer_par": layers, "gains": gains, "gates": np.ascontiguousarray(gates),
        "pool_mat": pool, "scale_row": np.ascontiguousarray(np.broadcast_to(i["od_scale"][0], (P, D))),
        "x_in": i["x"][0], "mem1": i["mem"][0], "mem2": i["mem_2"][0],
        "pos": np.ascontiguousarray(i["positions_2"][0].reshape(NT, P).T),
    }


def kernel(**inputs):
    import concourse.bacc as bacc
    from concourse.bass_utils import run_bass_kernel_spmd

    arrays = _layout({k: np.asarray(v) for k, v in inputs.items()})
    steps = {}
    for attempt in range(2):
        nc = bacc.Bacc("TRN2", target_bir_lowering=False, num_devices=1)
        args = {n: nc.dram_tensor(f"{n}_dram", a.shape, mybir.dt.from_np(a.dtype), kind="ExternalInput").ap()
                for n, a in arrays.items()}
        out = nc.dram_tensor("out_dram", (S, D), F32, kind="ExternalOutput").ap()
        build_program(nc, steps, out=out, **args)
    r = run_bass_kernel_spmd(nc, [{f"{n}_dram": a for n, a in arrays.items()}], core_ids=[0])
    return r.results[0]["out_dram"].reshape(1, S, D)
```
